# Optimizing a Trainium2 kernel written in Bass

```python
import jax, jax.numpy as jnp
from jax import lax
import numpy as np

D_MODEL = 1024
BATCH = 1
SEQ = 512
DEPTH = 1
DEC_BATCH = 8
DEC_SEQ = 1
PAST_LEN = 2048
PAGE_SIZE = 128

D_CONV = 512
CONV_W = 3
N_HEADS = 8
KV_HEADS = 2
HPG = N_HEADS // KV_HEADS
HEAD_DIM = 64
D_ATTN = N_HEADS * HEAD_DIM
KV_ROW = 2 * KV_HEADS * HEAD_DIM
CMP_STRIDE = 16
CMP_RATIO = 2
CMP_BLK = CMP_STRIDE * CMP_RATIO
CMP_HID = 128
SEL_BLK = 64
TOP_N = 16
WINDOW = 512
N_BRANCH = 3
D_FF = 2816
ROPE_THETA = 10000.0
EPS = 1e-6
Q_BLK = 64
NEG = -1e30
BIG = 1e9
IN_SPLITS = (D_CONV, D_CONV, D_CONV, D_ATTN, KV_ROW, KV_ROW, KV_ROW, N_HEADS * N_BRANCH, 2 * D_MODEL)
N_IN = sum(IN_SPLITS)

kernel_name = 'macaron_shortconv_nsa_hybrid_step'

def rmsnorm(x, g):
    xf = x.astype(jnp.float32)
    y = xf * lax.rsqrt(jnp.mean(xf * xf, axis=-1, keepdims=True) + EPS)
    return (y * g.astype(jnp.float32)).astype(x.dtype)

def half_ffn(x, g, w_gate, w_up, w_down):
    h = rmsnorm(x, g)
    return x + 0.5 * ((jax.nn.silu(h @ w_gate) * (h @ w_up)) @ w_down)

def rope(x, pos):
    half = HEAD_DIM // 2
    freqs = jnp.power(ROPE_THETA, -jnp.arange(half, dtype=jnp.float32) * (2.0 / HEAD_DIM))
    ang = pos.astype(jnp.float32)[:, None] * freqs[None, :]
    cos = jnp.cos(ang)[:, None, :]
    sin = jnp.sin(ang)[:, None, :]
    xf = x.astype(jnp.float32)
    x1, x2 = xf[..., :half], xf[..., half:]
    return jnp.concatenate([x1 * cos - x2 * sin, x1 * sin + x2 * cos], axis=-1).astype(x.dtype)

def mixer_front(h, w_mix_in, pos):
    b_, t_ = h.shape[:2]
    z = h @ w_mix_in
    offs = np.cumsum(IN_SPLITS)[:-1].tolist()
    u_b, u_c, u_x, q, kv_c, kv_s, kv_w, g_n, g_b = jnp.split(z, offs, axis=-1)
    q = rope(q.reshape(b_, t_, N_HEADS, HEAD_DIM), pos).reshape(b_, t_, KV_HEADS, HPG, HEAD_DIM)

    def rows(kv):
        kv = kv.reshape(b_, t_, 2, KV_HEADS, HEAD_DIM)
        return jnp.stack([rope(kv[:, :, 0], pos), kv[:, :, 1]], axis=2)

    g_n = jax.nn.sigmoid(g_n.reshape(b_, t_, KV_HEADS, HPG, N_BRANCH))
    g_b = jax.nn.sigmoid(g_b.reshape(b_, t_, 2, D_MODEL))
    return u_b, u_c * u_x, q, rows(kv_c), rows(kv_s), rows(kv_w), g_n, g_b

def short_conv(u, w, prev):
    ext = jnp.concatenate([prev.astype(u.dtype), u], axis=1)
    t_ = u.shape[1]
    y = w[0] * ext[:, 0:t_]
    for k in range(1, CONV_W):
        y = y + w[k] * ext[:, k:k + t_]
    return y, ext[:, t_:]

def compress(rows, w1, w2, pe):
    b_, l_ = rows.shape[:2]
    n_chunks = l_ // CMP_STRIDE
    n_cmp = n_chunks - CMP_RATIO + 1
    chunks = rows[:, :n_chunks * CMP_STRIDE].reshape(b_, n_chunks, CMP_STRIDE, KV_HEADS, HEAD_DIM)
    part = jnp.einsum('bcsgd,rsdh->bcrgh', chunks, w1)
    hid = jnp.einsum('rsd,rsdh->h', pe.reshape(CMP_RATIO, CMP_STRIDE, HEAD_DIM), w1)
    for r in range(CMP_RATIO):
        hid = hid + part[:, r:r + n_cmp, r]
    return jax.nn.silu(hid) @ w2

def cmp_ends(n_cmp):
    return jnp.arange(n_cmp, dtype=jnp.int32) * CMP_STRIDE + (CMP_BLK - 1)

def cmp_to_sel(n_cmp, n_sel):
    start = jnp.arange(n_cmp, dtype=jnp.int32)[:, None] * CMP_STRIDE
    jb = jnp.arange(n_sel, dtype=jnp.int32)[None, :] * SEL_BLK
    return ((start < jb + SEL_BLK) & (start + CMP_BLK > jb)).astype(jnp.float32)

def key_summaries(rows_cmp, rows_sel, w_cmpk1, w_cmpk2, pe_cmpk, w_cmpv1, w_cmpv2, pe_cmpv):
    kc = compress(rows_cmp[:, :, 0], w_cmpk1, w_cmpk2, pe_cmpk)
    vc = compress(rows_cmp[:, :, 1], w_cmpv1, w_cmpv2, pe_cmpv)
    b_, l_ = rows_sel.shape[:2]
    n_sel = -(-l_ // SEL_BLK)
    padded = jnp.pad(rows_sel, ((0, 0), (0, n_sel * SEL_BLK - l_), (0, 0), (0, 0), (0, 0)))
    blk = padded.reshape(b_, n_sel, SEL_BLK, 2, KV_HEADS, HEAD_DIM).transpose(3, 0, 4, 1, 2, 5)
    return kc, vc, blk[0], blk[1]

def nsa_core(q, t, kc, vc, kb, vb, kw, vw, kw_pos, gates):
    scale = HEAD_DIM ** -0.5
    n_cmp = kc.shape[1]
    n_sel = kb.shape[2]
    s = jnp.einsum('btghd,bngd->btghn', q, kc).astype(jnp.float32) * scale
    m = (cmp_ends(n_cmp)[None, :] <= t[:, None])[None, :, None, None, :]
    p_cmp = jax.nn.softmax(jnp.where(m, s, NEG), axis=-1) * m
    o_cmp = jnp.einsum('btghn,bngd->btghd', p_cmp.astype(vc.dtype), vc)
    imp = jnp.einsum('btghn,nj->btgj', p_cmp, cmp_to_sel(n_cmp, n_sel))
    j = jnp.arange(n_sel, dtype=jnp.int32)[None, :]
    cur = (t // SEL_BLK)[:, None]
    valid = j <= cur
    forced = valid & ((j == 0) | (j == cur) | (j == cur - 1))
    score = jnp.where(forced[None, :, None, :], BIG, jnp.where(valid[None, :, None, :], imp, -BIG))
    _, idx = lax.top_k(score, min(TOP_N, n_sel))
    bi = jnp.arange(q.shape[0])[:, None, None, None]
    gi = jnp.arange(KV_HEADS)[None, None, :, None]
    kg = kb[bi, gi, idx]
    vg = vb[bi, gi, idx]
    kpos = idx[..., None] * SEL_BLK + jnp.arange(SEL_BLK, dtype=jnp.int32)
    ms = (kpos <= t[None, :, None, None, None])[:, :, :, None]
    s = jnp.einsum('btghd,btgnkd->btghnk', q, kg).astype(jnp.float32) * scale
    s = jnp.where(ms, s, NEG)
    sh = s.shape
    p = jax.nn.softmax(s.reshape(sh[:-2] + (sh[-2] * sh[-1],)), axis=-1).reshape(sh)
    o_sel = jnp.einsum('btghnk,btgnkd->btghd', p.astype(vg.dtype), vg)
    s = jnp.einsum('btghd,bkgd->btghk', q, kw).astype(jnp.float32) * scale
    mw = (kw_pos[None, :] <= t[:, None]) & (kw_pos[None, :] > t[:, None] - WINDOW) & (kw_pos[None, :] >= 0)
    p = jax.nn.softmax(jnp.where(mw[None, :, None, None, :], s, NEG), axis=-1)
    o_win = jnp.einsum('btghk,bkgd->btghd', p.astype(vw.dtype), vw)
    return gates[..., 0:1] * o_cmp + gates[..., 1:2] * o_sel + gates[..., 2:3] * o_win

def mixer_merge(u_b, conv_y, o_attn, g_b, w_conv_out, w_attn_out, w_mix_out):
    y_c = (u_b * conv_y) @ w_conv_out
    y_a = o_attn @ w_attn_out
    return (g_b[:, :, 0] * y_c + g_b[:, :, 1] * y_a) @ w_mix_out

def mixer_prompt(h, w_mix_in, conv_w, w_cmpk1, w_cmpk2, pe_cmpk, w_cmpv1, w_cmpv2, pe_cmpv,
                 w_conv_out, w_attn_out, w_mix_out):
    b_, t_ = h.shape[:2]
    pos = jnp.arange(t_, dtype=jnp.int32)
    u_b, u_in, q, r_cmp, r_sel, r_win, g_n, g_b = mixer_front(h, w_mix_in, pos)
    conv_y, conv_state = short_conv(u_in, conv_w, jnp.zeros((b_, CONV_W - 1, D_CONV), h.dtype))
    kc, vc, kb, vb = key_summaries(r_cmp, r_sel, w_cmpk1, w_cmpk2, pe_cmpk, w_cmpv1, w_cmpv2, pe_cmpv)
    win_pad = jnp.pad(r_win, ((0, 0), (WINDOW, 0), (0, 0), (0, 0), (0, 0)))
    n_qb = t_ // Q_BLK
    qb = q.reshape(b_, n_qb, Q_BLK, KV_HEADS, HPG, HEAD_DIM).swapaxes(0, 1)
    gb = g_n.reshape(b_, n_qb, Q_BLK, KV_HEADS, HPG, N_BRANCH).swapaxes(0, 1)

    def block(args):
        q_i, g_i, i = args
        start = i * Q_BLK
        t = start + jnp.arange(Q_BLK, dtype=jnp.int32)
        w = lax.dynamic_slice_in_dim(win_pad, start, Q_BLK + WINDOW, axis=1)
        w_pos = start - WINDOW + jnp.arange(Q_BLK + WINDOW, dtype=jnp.int32)
        return nsa_core(q_i, t, kc, vc, kb, vb, w[:, :, 0], w[:, :, 1], w_pos, g_i)

    o = lax.map(block, (qb, gb, jnp.arange(n_qb, dtype=jnp.int32)))
    o = o.swapaxes(0, 1).reshape(b_, t_, D_ATTN)
    out = mixer_merge(u_b, conv_y, o, g_b, w_conv_out, w_attn_out, w_mix_out)
    return out, r_cmp, r_sel, r_win[:, t_ - min(WINDOW, t_):], conv_state

def mixer_sample(h, cache_cmp, cache_sel, win_buf, conv_buf, page_table, w_mix_in, conv_w,
                 w_cmpk1, w_cmpk2, pe_cmpk, w_cmpv1, w_cmpv2, pe_cmpv, w_conv_out, w_attn_out, w_mix_out):
    b_, s_ = h.shape[:2]
    pos = PAST_LEN + jnp.arange(s_, dtype=jnp.int32)
    u_b, u_in, q, r_cmp, r_sel, r_win, g_n, g_b = mixer_front(h, w_mix_in, pos)
    conv_y, conv_state = short_conv(u_in, conv_w, conv_buf)
    past_cmp = cache_cmp[page_table].reshape(b_, -1, 2, KV_HEADS, HEAD_DIM)
    past_sel = cache_sel[page_table].reshape(b_, -1, 2, KV_HEADS, HEAD_DIM)
    kc, vc, kb, vb = key_summaries(jnp.concatenate([past_cmp, r_cmp.astype(past_cmp.dtype)], axis=1),
                                   jnp.concatenate([past_sel, r_sel.astype(past_sel.dtype)], axis=1),
                                   w_cmpk1, w_cmpk2, pe_cmpk, w_cmpv1, w_cmpv2, pe_cmpv)
    w_all = jnp.concatenate([win_buf, r_win.astype(win_buf.dtype)], axis=1)
    w_buf = win_buf.shape[1]
    w_pos = PAST_LEN - w_buf + jnp.arange(w_buf + s_, dtype=jnp.int32)
    o = nsa_core(q, pos, kc, vc, kb, vb, w_all[:, :, 0], w_all[:, :, 1], w_pos, g_n).reshape(b_, s_, D_ATTN)
    out = mixer_merge(u_b, conv_y, o, g_b, w_conv_out, w_attn_out, w_mix_out)
    return out, r_cmp, r_sel, w_all[:, s_:], conv_state

def setup_inputs(seed: int = 0) -> dict:
    key = jax.random.key(seed)
    k = jax.random.split(key, 32)

    def nrm(i, shape, scale):
        return jax.random.normal(k[i], shape, jnp.float32) * scale

    n_pages = PAST_LEN // PAGE_SIZE
    n_used = DEC_BATCH * n_pages
    n_phys = n_used + (n_used + 3) // 4
    w_buf = min(WINDOW, PAST_LEN)
    L = DEPTH
    page_table = jax.random.permutation(k[2], n_phys)[:n_used].reshape(DEC_BATCH, n_pages).astype(jnp.int32)
    return {
        'x_prompt': nrm(0, (BATCH, SEQ, D_MODEL), 1.0),
        'x_sample': nrm(1, (DEC_BATCH, DEC_SEQ, D_MODEL), 1.0),
        'cache_cmp_kv': nrm(3, (L, n_phys, PAGE_SIZE, 2, KV_HEADS, HEAD_DIM), 1.0),
        'cache_sel_kv': nrm(4, (L, n_phys, PAGE_SIZE, 2, KV_HEADS, HEAD_DIM), 1.0),
        'state_win_kv': nrm(5, (L, DEC_BATCH, w_buf, 2, KV_HEADS, HEAD_DIM), 1.0),
        'state_conv': nrm(6, (L, DEC_BATCH, CONV_W - 1, D_CONV), 1.0),
        'page_table': page_table,
        'norm_ffn1': 1.0 + nrm(7, (L, D_MODEL), 0.05),
        'ffn1_w_gate': nrm(8, (L, D_MODEL, D_FF), D_MODEL ** -0.5),
        'ffn1_w_up': nrm(9, (L, D_MODEL, D_FF), D_MODEL ** -0.5),
        'ffn1_w_down': nrm(10, (L, D_FF, D_MODEL), D_FF ** -0.5),
        'norm_mix': 1.0 + nrm(11, (L, D_MODEL), 0.05),
        'w_mix_in': nrm(12, (L, D_MODEL, N_IN), D_MODEL ** -0.5),
        'conv_w': nrm(13, (L, CONV_W, D_CONV), CONV_W ** -0.5),
        'w_cmpk1': nrm(14, (L, CMP_RATIO, CMP_STRIDE, HEAD_DIM, CMP_HID), (CMP_BLK * HEAD_DIM) ** -0.5),
        'w_cmpk2': nrm(15, (L, CMP_HID, HEAD_DIM), CMP_HID ** -0.5),
        'pe_cmpk': nrm(16, (L, CMP_BLK, HEAD_DIM), 0.1),
        'w_cmpv1': nrm(17, (L, CMP_RATIO, CMP_STRIDE, HEAD_DIM, CMP_HID), (CMP_BLK * HEAD_DIM) ** -0.5),
        'w_cmpv2': nrm(18, (L, CMP_HID, HEAD_DIM), CMP_HID ** -0.5),
        'pe_cmpv': nrm(19, (L, CMP_BLK, HEAD_DIM), 0.1),
        'w_conv_out': nrm(20, (L, D_CONV, D_MODEL), D_CONV ** -0.5),
        'w_attn_out': nrm(21, (L, D_ATTN, D_MODEL), D_ATTN ** -0.5),
        'w_mix_out': nrm(22, (L, D_MODEL, D_MODEL), D_MODEL ** -0.5),
        'norm_ffn2': 1.0 + nrm(23, (L, D_MODEL), 0.05),
        'ffn2_w_gate': nrm(24, (L, D_MODEL, D_FF), D_MODEL ** -0.5),
        'ffn2_w_up': nrm(25, (L, D_MODEL, D_FF), D_MODEL ** -0.5),
        'ffn2_w_down': nrm(26, (L, D_FF, D_MODEL), D_FF ** -0.5),
        'norm_final': 1.0 + nrm(27, (D_MODEL,), 0.05),
    }

def reference(x_prompt, x_sample, cache_cmp_kv, cache_sel_kv, state_win_kv, state_conv, page_table,
              norm_ffn1, ffn1_w_gate, ffn1_w_up, ffn1_w_down, norm_mix, w_mix_in, conv_w,
              w_cmpk1, w_cmpk2, pe_cmpk, w_cmpv1, w_cmpv2, pe_cmpv, w_conv_out, w_attn_out, w_mix_out,
              norm_ffn2, ffn2_w_gate, ffn2_w_up, ffn2_w_down, norm_final):
    xp, xs = x_prompt, x_sample
    cmp_p, sel_p, win_p, conv_p = [], [], [], []
    cmp_s, sel_s, win_s, conv_s = [], [], [], []
    for l in range(DEPTH):
        mw = (w_mix_in[l], conv_w[l], w_cmpk1[l], w_cmpk2[l], pe_cmpk[l], w_cmpv1[l], w_cmpv2[l], pe_cmpv[l],
              w_conv_out[l], w_attn_out[l], w_mix_out[l])
        xp = half_ffn(xp, norm_ffn1[l], ffn1_w_gate[l], ffn1_w_up[l], ffn1_w_down[l])
        xs = half_ffn(xs, norm_ffn1[l], ffn1_w_gate[l], ffn1_w_up[l], ffn1_w_down[l])
        mp, rc, rs, rw, rv = mixer_prompt(rmsnorm(xp, norm_mix[l]), *mw)
        cmp_p.append(rc); sel_p.append(rs); win_p.append(rw); conv_p.append(rv)
        ms, rc, rs, rw, rv = mixer_sample(rmsnorm(xs, norm_mix[l]), cache_cmp_kv[l], cache_sel_kv[l],
                                          state_win_kv[l], state_conv[l], page_table, *mw)
        cmp_s.append(rc); sel_s.append(rs); win_s.append(rw); conv_s.append(rv)
        xp = xp + mp
        xs = xs + ms
        xp = half_ffn(xp, norm_ffn2[l], ffn2_w_gate[l], ffn2_w_up[l], ffn2_w_down[l])
        xs = half_ffn(xs, norm_ffn2[l], ffn2_w_gate[l], ffn2_w_up[l], ffn2_w_down[l])
    y_prompt = rmsnorm(xp, norm_final)
    y_sample = rmsnorm(xs, norm_final)
    return (y_prompt, y_sample, jnp.stack(cmp_p), jnp.stack(sel_p), jnp.stack(win_p), jnp.stack(conv_p),
            jnp.stack(cmp_s), jnp.stack(sel_s), jnp.stack(win_s), jnp.stack(conv_s))


_drawn_inputs = setup_inputs


def setup_inputs(seed=0):
    import zlib

    import numpy as np

    out = dict(_drawn_inputs(seed))
    spreads = {}
    factors = {'cache_cmp_kv': 3.004,
     'cache_sel_kv': 4.13,
     'pe_cmpk': 8.0,
     'pe_cmpv': 3.547,
     'norm_ffn2': 3.285}
    for name, (base, spread) in spreads.items():
        noise = np.random.default_rng([zlib.crc32(name.encode()), seed]).standard_normal(out[name].shape)
        drawn = base * np.exp(spread * noise) if base else spread * noise
        out[name] = __import__('jax').numpy.asarray(drawn.astype(out[name].dtype))
    for name, factor in factors.items():
        out[name] = (out[name] * factor).astype(out[name].dtype)
    return out
```

```python
from contextlib import ExitStack

import numpy as np

import concourse.bass as bass
from concourse import mybir

F32 = mybir.dt.float32
F32R = mybir.dt.float32r
I32 = mybir.dt.int32
U32 = mybir.dt.uint32
ALU = mybir.AluOpType
ACT = mybir.ActivationFunctionType
AX = mybir.AxisListType

P = 128
D = 1024
SEQ = 512
DB = 8
T = SEQ + DB
HT = T // 2
DC = D // P
DFF = 2816
DFC = DFF // P
PAST = 2048
PAGE = 128
CH = 16
NCH = PAST // CH
NCMP = NCH - 1
PCH = SEQ // CH
PCMP = PCH - 1
HD = 64
NH = 8
KVH = 2
HPG = NH // KVH
ROW = 2 * KVH * HD
DCV = 512
NSEL = PAST // 64 + 1
TOP = 16
EPS = 1e-6
BIG = 1e9
NEG = -1e30
SCALE = HD ** -0.5
C_Q = 3 * DCV
C_KV = C_Q + NH * HD
C_GN = C_KV + 3 * ROW
C_GB = C_GN + NH * 3
QT = SEQ // P
WS = 4
KA = 12
KB = DFC - KA

FFN_UNITS = 2 * DFC + 2 * DC
U_F1, U_M1 = 0, FFN_UNITS
U_M3 = U_M1 + 23
U_M4 = U_M3 + 32
U_F2 = U_M4 + 8
U_END = U_F2 + FFN_UNITS
L_F1, L_M1 = 0, FFN_UNITS // 2
L_M3 = L_M1 + 12
L_M4 = L_M3 + 16
L_F2 = L_M4 + 4
G_X = 0
G_ST = [DC, DC + 1 + FFN_UNITS, U_F2 + DC + 2]
OFF_F1, OFF_M, OFF_F2 = DC + 1, DC + 2, DC + 3


def phase_of(u):
    for base in (U_F1, U_F2):
        if base <= u < base + FFN_UNITS:
            v = u - base
            return DC if v < 24 else KA if v < 32 else DC if v < 52 else KB
    if U_M3 <= u < U_M4:
        return DC if (u - U_M3) % 8 < 4 else 4
    return DC


def group(u):
    return u + (OFF_F1 if u < U_M1 else OFF_M if u < U_F2 else OFF_F2)


def load_of(u):
    if u < U_M3:
        return u // 2, u % 2
    return L_M3 + (u - U_M3) // 2, (u - U_M3) % 2


def load_unit(n):
    return 2 * n if n < L_M3 else U_M3 + 2 * (n - L_M3)


def load_incs(n):
    if n in (L_M1 + 6, L_M1 + 7):
        return 32
    if L_M3 <= n < L_M4 and (n - L_M3) % 4 == 3:
        return 32
    return 16


def raw_count(n):
    return sum(load_incs(k) for k in range(n % 2, n + 1, 2))


def build(nc, a):
    with ExitStack() as ctx:
        base = 16512

        def at(name, off, shape, dt=F32):
            return nc.alloc_sbuf_tensor_at(name, shape, dt, offset=base + off)

        def sem(name):
            return ctx.enter_context(nc.semaphore(name))

        CHB = T * 4
        X0, W0, T0 = 0, 3 * DC * CHB, 3 * DC * CHB + 2 * 12288 + 2 * 24576
        C0 = T0 + 8 * CHB
        xT = at("xT", X0, [P, DC, T])
        xh = at("xh", X0 + DC * CHB, [P, DC, T], F32R)
        xl = at("xl", X0 + 2 * DC * CHB, [P, DC, T], F32R)
        xg = at("xg", X0 + DC * CHB, [P, DC, T])
        raw = [at(f"raw{s}", W0 + 12288 * s, [P, KA, 2 * P]) for s in range(2)]
        whi = at("whi", W0 + 24576, [P, WS, KA, P], F32R)
        wlo = at("wlo", W0 + 49152, [P, WS, KA, P], F32R)
        tmp = [at(f"tmp{k}", T0 + CHB * k, [P, T]) for k in range(8)]
        ssq = tmp[7]
        o = [C0]

        def small(name, shape, dt=F32):
            n = int(np.prod(shape[1:])) * 4
            t = at(name, o[0], shape, dt)
            o[0] += (n + 31) // 32 * 32
            return t

        ident = small("ident", [P, P])
        ones = small("ones", [P, P])
        cs = small("cs", [P, 2, T])
        srows = at("srows", C0 + 1024, [DB, 3 * ROW])
        tri = small("tri", [P, SEQ])
        kcS = small("kcS", [P, DB, NCMP])
        vcS = small("vcS", [NCMP, DB, P])
        rr = small("rr", [P, T])
        gn4 = small("gn4", [P, 4, DC])
        cw = small("cw", [P, 3, 4])
        sc = small("sc", [P, 4, 2, DB])
        tail = small("tail", [P, 4, 10])
        w2 = small("w2", [P, 2, HD])
        hpe = small("hpe", [P, 2])
        idx = small("idx", [P, DB], U32)
        ptab = small("ptab", [P, DB], I32)
        sub = small("sub", [P, 1])
        gt = small("gt", [P, QT, 24])
        gts = small("gts", [DB, 24])
        g64 = small("g64", [64, 3])
        valid = small("valid", [P, QT])
        cmask = small("cmask", [P, QT, PCMP])
        mcs = small("mcs", [NCMP, NSEL])
        e16 = small("e16", [16, 64])
        e8 = small("e8", [DB, 64])
        dmask = small("dmask", [64, DB * KVH])
        gmask = small("gmask", [64, KVH])
        kcP = small("kcP", [P, PCMP])
        vcP = small("vcP", [PCMP, P])
        st5 = small("st5", [P, 5])
        nmx = small("nmx", [P, 2, QT])
        lsm = small("lsm", [P, 2, QT])
        fct = small("fct", [P, 2, QT])
        cmx = small("cmx", [P, 2, QT])
        cfc = small("cfc", [P, 2, QT])
        sst = small("sst", [64, 16])
        bump = small("bump", [P, 4])
        A0 = (o[0] + 31) // 32 * 32
        HB = KA * CHB
        hh = at("hh", A0, [P, KA, T], F32R)
        hl = at("hl", A0 + HB, [P, KA, T], F32R)
        assert base + A0 + 2 * HB <= 229344, base + A0 + 2 * HB
        ub = at("ub", A0, [P, 4, T])
        ui = at("ui", A0 + 4 * CHB, [P, 4, T])
        vch = at("vch", A0, [P, 4, T], F32R)
        vcl = at("vcl", A0 + 4 * CHB, [P, 4, T], F32R)
        Q = at("Q", A0 + 8 * CHB, [P, 4, T])
        otl = at("otl", A0 + 8 * CHB, [P, 4, T], F32R)
        kv = at("kv", A0 + 12 * CHB, [P, 6, T])
        oth = at("oth", A0 + 12 * CHB, [P, 4, T], F32R)
        rows = at("rows", A0 + 18 * CHB, [P, QT, 3 * ROW])
        mm = at("mm", A0 + 16 * CHB, [P, DC, T])
        mh = at("mh", A0, [P, DC, T], F32R)
        ml = at("ml", A0 + 8 * CHB, [P, DC, T], F32R)
        XC = [at(f"XC{k}", X0 + 16384 * k, [NCH, CH, ROW]) for k in range(2)]
        XT = [at("XTk", X0 + 32768, [P, 8, 4, NCH]), at("XTv", A0, [P, 8, 4, NCH])]
        w1 = at("w1", A0 + 16384, [P, 2, 16, P])
        xr = at("xr", A0 + 32768, [P, QT, D])
        xrs = at("xrs", T0, [DB, D])
        SH = [at(f"SH{k}", T0 + 4096 + 2048 * k, [P, 4, NCMP]) for k in range(2)]
        per = at("per", T0 + 8192, [16, 2, P])
        pet = at("pet", T0 + 9216, [P, 2, 16])
        scr = at("scr", T0 + 10240, [DB, 2 * DCV])
        GB = [at(f"GB{k}", W0 + 16384 * k, [NCH, CH, ROW]) for k in range(2)]
        xcp = at("xcp", W0, [PCH, CH, ROW])
        w1p = at("w1p", W0 + 16384, [P, 2, 16, P])
        NPS = PAST + 1 + SEQ + P
        ps = at("ps", W0 + 32768, [64, NPS])
        pst = at("pst", W0 + 43648, [P, 21, 64])
        sm = [at(f"sm{k}", W0 + 49152 + 5120 * k, [P, QT * (QT + 1) // 2 * P]) for k in range(2)]
        ptp = at("ptp", W0 + 59392, [P, QT, SEQ])
        kt = [at(f"kt{k}", W0 + 67584 + 2048 * k, [P, SEQ]) for k in range(2)]
        xtp = [at(f"xtp{k}", W0 + 67584 + 2048 * k, [P, 8, KVH, PCH]) for k in range(2)]
        qp = at("qp", A0 + 12 * CHB, [P, DB, 72])
        wt = [at(f"wt{k}", T0 + 4096 * k, [P, 4, ROW]) for k in range(2)]
        qz = at("qz", T0 + 4 * CHB, [P, KVH, SEQ])
        ptc = at("ptc", T0 + 6 * CHB, [PCMP, SEQ])
        cm = [at(f"cm{k}", T0 + 7 * CHB + 512 * k, [P, QT, PCMP]) for k in range(2)]
        scs = at("scs", T0 + 7 * CHB + 1024, [64, 132])
        qps = [at(f"qps{k}", T0 + 7 * CHB + 1568 + 256 * k, [P, 64]) for k in range(2)]
        pcS = at("pcS", W0 + 49152, [NCMP, 16])
        scr16 = at("scr16", W0 + 49216, [16, NSEL])
        rk16 = at("rk16", W0 + 49376, [16, NSEL])
        cmp3 = at("cmp3", W0 + 59392, [16, NSEL, NSEL])
        eq3 = at("eq3", W0 + 49984, [16, NSEL, NSEL])
        tie3 = at("tie3", W0 + 54368, [16, NSEL, NSEL])
        sb64 = at("sb64", W0 + 49536, [64, NSEL])
        shp = [at(f"shp{k}", T0 + 10400 + 256 * k, [P, KVH * PCMP]) for k in range(2)]
        trow = at("trow", T0 + 4 * CHB, [10, DCV])
        gnT = at("gnT", T0 + 7 * CHB, [24, T])
        zz = at("zz", W0 + 49696, [P, 64])
        om = at("om", W0 + 67584, [64, DB, P])
        o64 = at("o64", W0 + 49152 + 4096, [64, P])
        o64b = at("o64b", W0 + 49152 + 4608, [64, P])
        oS = at("oS", W0 + 49152 + 5376, [P, 32])
        oT64 = at("oT64", W0 + 49152 + 5120, [P, 64])
        yr = [at(f"yr{k}", A0 + 4096 * k, [P, D]) for k in range(QT + 1)]

        bank = ctx.enter_context(nc.psum_tensor("bank", [P, 8, 512], F32))

        def acc(g):
            return bank[:, 2 * (g % WS):2 * (g % WS) + 2, 0:HT]

        def flat(g, n, p=P):
            return bank[0:p, 2 * (g % WS):2 * (g % WS) + 2, :].rearrange("p a b -> p (a b)")[:, 0:n]

        def two(t):
            return t.rearrange("p (a b) -> p a b", a=2)

        def halves(xt, s, bk):
            half = slice(HD * (s % 2), HD * (s % 2) + HD)
            dst = xt[half, s // 2 * 2:s // 2 * 2 + 2, :, :].rearrange("p s (b g) c -> p s b g c", g=KVH)
            for g in range(KVH):
                yield dst[:, :, :, g, :], bank[HD * g:HD * (g + 1), bk, :].rearrange("p (s b c) -> p s b c", s=2, b=2)

        gscr = nc.dram_tensor("gate_scratch", [DB, 24], F32, kind="Internal").ap()

        ident_loaded, const_loaded, ptab_loaded, cmpw_loaded, x_loaded = map(sem, ("ident_loaded", "const_loaded", "ptab_loaded", "cmpw_loaded", "x_loaded"))
        raw_loaded = [sem("raw0_loaded"), sem("raw1_loaded")]
        idx_ready = sem("idx_ready")
        xc_loaded = [sem("xc0_loaded"), sem("xc1_loaded")]
        gb_loaded = [sem("gb0_loaded"), sem("gb1_loaded")]
        xt_a, xt_d, xt_ev_a, xt_ev_d = map(sem, ("xt_turned_a", "xt_turned_d", "xt_emptied_a", "xt_emptied_d"))
        hid_done, hid_act, cmp_done, cmp_ev = map(sem, ("hid_done", "hid_act", "cmp_done", "cmp_emptied"))
        pe_tp, pe_ev, hpe_done, hpe_ready = map(sem, ("pe_turned", "pe_emptied", "hpe_done", "hpe_ready"))
        hi_done, lo_done, grp_done, acc_free = map(sem, ("hi_done", "lo_done", "grp_done", "acc_free"))
        xh_done, xl_done, x_step, ssq_ready, std_ready, r_ready = map(
            sem, ("xh_done", "xl_done", "x_step", "ssq_ready", "std_ready", "r_ready"))
        silu_done, h_ready, hh_done, hl_done = map(sem, ("silu_done", "h_ready", "hh_done", "hl_done"))
        m_step, kv_ready, v_ready, vch_done, vcl_done, gn_sig = map(
            sem, ("m_step", "kv_ready", "v_ready", "vch_done", "vcl_done", "gn_sig"))
        sc_ready = sem("sc_ready")
        tp_done, tp_ev = sem("tp_done"), sem("tp_emptied")
        out_s, win_s, gscr_s, g64_loaded, xcp_loaded, w1p_loaded, tie_loaded = map(
            sem, ("out_stored", "win_stored", "gate_scratch_stored", "g64_loaded", "xcp_loaded", "w1p_loaded", "tie_loaded"))
        cph_done, cph_act, cpo_done, cpo_ev = map(sem, ("cph_done", "cph_act", "cpo_done", "cpo_emptied"))
        qp_ready, scm_done, scs_ready, sc_nm, sc_exp, pcn_ready, pct_done, pcs_ready, imp_done, selb_ready, selx_done = map(
            sem, ("qp_ready", "score_cmp_done", "scs_ready", "sc_nm", "sc_exp", "pcn_ready", "pct_done", "pcs_ready",
                  "imp_done", "selb_ready", "selx_done"))
        s_step, qps_ready, kt_used, zz_ready = map(sem, ("s_step", "qps_ready", "kt_used", "zz_ready"))
        wt_loaded = [sem("wt0_loaded"), sem("wt1_loaded")]
        snm, sexp, ps_ready = map(sem, ("sample_nm", "sample_exp", "ps_ready"))
        qz_ready, big_s, cmp_s, big_rd, cmp_rd, big_nm, big_exp, big_p, cmp_nm, cmp_exp, cmp_p, pv_done, o_hi, o_lo, p_step = map(
            sem, ("qz_ready", "big_scores", "cmp_scores", "big_read", "cmp_read", "big_nm", "big_exp", "big_p",
                  "cmp_nm", "cmp_exp", "cmp_p", "pv_done", "o_hi", "o_lo", "p_step"))
        sv_done, sv_rd, vn_done, o64_ready, o64_tp, os_hi = map(sem, ("sample_pv", "sample_pv_read", "vnew_done", "o64_ready", "o64_turned", "os_hi"))
        os_lo, ones_ready, gt_ready, mh_done, ml_done = map(sem, ("os_lo", "ones_ready", "gt_ready", "mh_done", "ml_done"))
        sig_done, m_ready = map(sem, ("sig_done", "m_ready"))
        fst_done, fms_ready, fstd_ready, fr_ready, xg_ready, y_tp, y_ev, y_out = map(
            sem, ("final_stats", "final_ms", "final_std", "final_r", "xg_ready", "y_turned", "y_emptied", "y_stored"))

        class Steps:

            def __init__(self, eng, s):
                self.eng, self.s, self.n, self.i, self.per = eng, s, 0, None, 0

            def did(self, ins):
                ins.then_inc(self.s, 1)
                self.n += 1
                return self.n

            def wait(self, n=None):
                n = self.n if n is None else n
                self.eng.wait_ge(self.s, n if self.i is None else n + self.i * self.per)

            def loop(self, i, per):
                self.i, self.per, self.first = i, per, self.n

            def end(self, times):
                assert self.n - self.first == self.per, (self.n - self.first, self.per)
                self.n = self.first + self.per * times
                self.i = None

        TB = 9
        TBS = TB + 40
        TBP = TBS + 3

        block = ctx.enter_context(nc.Block())

        @block.sync
        def _(sp):
            for r in range(8):
                sp.dma_start(ptab[r:P - 7 + r:8, :], a["page_table"].rearrange("b p -> p b"),
                             allow_slow_non_contiguous=True).then_inc(ptab_loaded, 16)
            sp.dma_start(sub[:, :], a["c_sub"]).then_inc(ptab_loaded, 16)
            sp.dma_start(ident[:, :], a["c_ident"]).then_inc(ident_loaded, 16)
            sp.dma_start(scr[:, :], a["state_conv"][0].rearrange("b k d -> b (k d)")).then_inc(cmpw_loaded, 16)
            for k, n in enumerate(("k", "v")):
                sp.dma_start(per[:, k, :], a[f"pe_cmp{n}"][0].rearrange("(j r) d -> j (r d)", r=2)).then_inc(cmpw_loaded, 16)
                sp.dma_start(w1[:, k, :, :], a[f"w_cmp{n}1"][0].rearrange("r s d h -> (r s d) h")
                             .rearrange("(j p) h -> p j h", p=P)).then_inc(cmpw_loaded, 16)
                sp.dma_start(w2[:, k, :], a[f"w_cmp{n}2"][0]).then_inc(cmpw_loaded, 16)
            for k, n in enumerate(("norm_ffn1", "norm_mix", "norm_ffn2", "norm_final")):
                src = a[n] if n == "norm_final" else a[n][0]
                sp.dma_start(gn4[:, k, :], src.rearrange("(c p) -> p c", p=P),
                             allow_slow_non_contiguous=True).then_inc(const_loaded, 16)
            for k in range(3):
                sp.dma_start(cw[:, k, :], a["conv_w"][0, k].rearrange("(c p) -> p c", p=P),
                             allow_slow_non_contiguous=True).then_inc(const_loaded, 16)
            for t, n in ((cmask, "c_cmask"), (tri, "c_tri"), (valid, "c_valid"), (mcs, "c_mcs"), (e16, "c_e16"),
                         (e8, "c_e8"), (dmask, "c_dmask"), (gmask, "c_gmask"), (cs, "c_cs")):
                sp.dma_start(t[:], a[n]).then_inc(const_loaded, 16)
            sp.dma_start(xr[:, :, :], a["x_prompt"][0].rearrange("(t p) d -> p t d", p=P)).then_inc(x_loaded, 16)
            sp.dma_start(xrs[:, :], a["x_sample"][:, 0, :]).then_inc(x_loaded, 16)

            def slot_free(n, i=None, units=0):
                if n < 2 and i is None:
                    return
                u = load_unit(n - 1) if i is None else load_unit(n) - 2
                sp.wait_ge(lo_done, u if i is None else u + i * units)

            def ffn_loads(n0, gate, up, down):
                for first, k, iters in ((0, KA, KA // 2), (KA, KB, KB // 2)):
                    for m in range(2):
                        slot_free(n0 + m)
                        sp.dma_start(raw[(n0 + m) % 2][:, 0:DC, :], (gate, up)[m][:, :, first * P:(first + 2) * P])\
                            .then_inc(raw_loaded[(n0 + m) % 2], 16)
                    with sp.Fori(1, iters) as i:
                        for m in range(2):
                            src = (gate, up)[m][:, :, first * P:][:, :, bass.ds(i * (2 * P), 2 * P)]
                            slot_free(n0 + m, i, 4)
                            sp.dma_start(raw[(n0 + m) % 2][:, 0:DC, :], src).then_inc(raw_loaded[(n0 + m) % 2], 16)
                    n0 += 2 * iters
                    rows_ = down[first * P:(first + k) * P, :].rearrange("(k p) n -> p k n", p=P)
                    for m in range(4):
                        slot_free(n0 + m)
                        sp.dma_start(raw[(n0 + m) % 2][:, 0:k, :], rows_[:, :, 2 * P * m:2 * P * (m + 1)])\
                            .then_inc(raw_loaded[(n0 + m) % 2], 16)
                    n0 += 4

            def kview(w):
                return w.rearrange("(k p) n -> p k n", p=P)

            ffn_loads(L_F1, kview(a["ffn1_w_gate"][0]), kview(a["ffn1_w_up"][0]), a["ffn1_w_down"][0])
            sp.dma_start(a["win_kv_sample"][0, :, 0:SEQ - 1], a["state_win_kv"][0, :, 1:SEQ]).then_inc(win_s, 16)
            sp.dma_start(a["conv_sample"][0, :, 0, :], a["state_conv"][0, :, 1, :]).then_inc(out_s, 16)
            wm = kview(a["w_mix_in"][0])
            for m in range(12):
                n = L_M1 + m
                slot_free(n)
                s = n % 2
                if m in (6, 7):
                    for g in range(KVH):
                        c = C_Q + g * HPG * HD + (m - 6) * P
                        sp.dma_start(raw[s][:, 0:DC, g * P:(g + 1) * P], wm[:, :, c:c + P]).then_inc(raw_loaded[s], 16)
                elif m < 11:
                    sp.dma_start(raw[s][:, 0:DC, :], wm[:, :, 2 * P * m:2 * P * (m + 1)]).then_inc(raw_loaded[s], 16)
                else:
                    sp.dma_start(raw[s][:, 0:DC, 0:24], wm[:, :, C_GN:C_GB]).then_inc(raw_loaded[s], 16)
            sp.wait_ge(tp_ev, 4)
            for r, nm in enumerate(("cmp_kv_prompt", "sel_kv_prompt", "win_kv_prompt")):
                sp.dma_start(a[nm].rearrange("l b (t p) c h d -> p (l b t) (c h d)", p=P),
                             rows[:, :, r * ROW:(r + 1) * ROW]).then_inc(xcp_loaded if r == 0 else out_s, 16)
            sp.wait_ge(grp_done, group(U_M3 - 1) + 1)
            for k, n in enumerate(("k", "v")):
                sp.dma_start(w1p[:, k, :, :], a[f"w_cmp{n}1"][0].rearrange("r s d h -> (r s d) h")
                             .rearrange("(j p) h -> p j h", p=P)).then_inc(w1p_loaded, 16)
            sp.dma_start(tie3[:], a["c_tie"]).then_inc(tie_loaded, 16)
            sp.wait_ge(xcp_loaded, 16)
            sp.dma_start(xcp[:], a["cmp_kv_prompt"].rearrange("l b (t s) c h d -> (l b t) s (c h d)", s=CH))\
                .then_inc(xcp_loaded, 16)
            sp.wait_ge(tp_ev, 5)
            for r, nm in enumerate(("cmp_kv_sample", "sel_kv_sample")):
                sp.dma_start(a[nm].rearrange("l b t c h d -> (l b t) (c h d)"), srows[:, r * ROW:(r + 1) * ROW])\
                    .then_inc(out_s, 16)
            sp.dma_start(a["win_kv_sample"][0, :, SEQ - 1].rearrange("b c h d -> b (c h d)"), srows[:, 2 * ROW:3 * ROW])\
                .then_inc(win_s, 16)
            sp.wait_ge(tp_ev, 6)
            sp.dma_start(a["conv_prompt"][0, 0], trow[0:2, :]).then_inc(out_s, 16)
            sp.dma_start(a["conv_sample"][0, :, 1, :], trow[2:10, :]).then_inc(out_s, 16)
            sp.wait_ge(tp_ev, 7)
            sp.dma_start(gscr, gts[:, :]).then_inc(gscr_s, 16)
            sp.wait_ge(gscr_s, 16)
            sp.dma_start(g64[:, :], gscr.rearrange("b (h c) -> (b h) c", c=3)).then_inc(g64_loaded, 16)
            sp.wait_ge(win_s, 32)
            wv = a["win_kv_sample"][0].rearrange("b (t p) c h d -> p b t (c h d)", p=P)
            for s in range(2):
                sp.dma_start(wt[s][:, :, :], wv[:, s, :, :]).then_inc(wt_loaded[s], 16)
            with sp.Fori(0, 3) as i:
                for s in range(2):
                    sp.wait_ge(tp_done, i * 10 + (TB + 5 * s + 5))
                    sp.dma_start(wt[s][:, :, :], wv[:, bass.ds(i * 2 + (2 + s), 1), :, :]
                                 .rearrange("p b t e -> p (b t) e")).then_inc(wt_loaded[s], 16)
            for s in range(2):
                sp.wait_ge(tp_done, TB + 30 + 5 * s + 5)
                sp.dma_start(wt[s][:, :, :], wv[:, s, :, :]).then_inc(wt_loaded[s], 16)
            with sp.Fori(0, 3) as i:
                for s in range(2):
                    sp.wait_ge(sv_done, i * 2 + (s + 1))
                    sp.dma_start(wt[s][:, :, :], wv[:, bass.ds(i * 2 + (2 + s), 1), :, :]
                                 .rearrange("p b t e -> p (b t) e")).then_inc(wt_loaded[s], 16)
            sp.wait_ge(sv_done, DB)
            wc = kview(a["w_conv_out"][0])
            wa = a["w_attn_out"][0].rearrange("(g j p) n -> g p j n", g=KVH, p=HD)

            def m3(i, n):
                def cols(w):
                    return w[:, :, 0:2 * P] if i is None else w[:, :, 2 * P:][:, :, bass.ds(i * (2 * P), 2 * P)]

                for m, w in enumerate((wm[:, :, C_GB:], wm[:, :, C_GB + D:], wc)):
                    src = cols(w)
                    slot_free(n + m, i, 8)
                    sp.dma_start(raw[(n + m) % 2][:, 0:DC if m < 2 else 4, :], src).then_inc(raw_loaded[(n + m) % 2], 16)
                s = (n + 3) % 2
                src = [cols(wa[g]) for g in range(KVH)]
                slot_free(n + 3, i, 8)
                for g in range(KVH):
                    sp.dma_start(raw[s][HD * g:HD * (g + 1), 0:4, :], src[g]).then_inc(raw_loaded[s], 16)

            m3(None, L_M3)
            with sp.Fori(0, 3) as i:
                m3(i, L_M3 + 4)
            wo = kview(a["w_mix_out"][0])
            for m in range(4):
                slot_free(L_M4 + m)
                sp.dma_start(raw[(L_M4 + m) % 2][:, 0:DC, :], wo[:, :, 2 * P * m:2 * P * (m + 1)])\
                    .then_inc(raw_loaded[(L_M4 + m) % 2], 16)
            ffn_loads(L_F2, kview(a["ffn2_w_gate"][0]), kview(a["ffn2_w_up"][0]), a["ffn2_w_down"][0])
            for t in range(QT + 1):
                sp.wait_ge(y_ev, t + 1)
                if t < QT:
                    sp.dma_start(a["y_prompt"][0, t * P:(t + 1) * P, :], yr[t][:, :]).then_inc(y_out, 16)
                else:
                    sp.dma_start(a["y_sample"][:, 0, :], yr[t][0:DB, :]).then_inc(y_out, 16)
            sp.wait_ge(y_out, 16 * (QT + 1))
            sp.wait_ge(out_s, 16 * 7)
            sp.wait_ge(win_s, 32)

        @block.gpsimd
        def _(pool):
            pool.memset(ones[:, :], 1.0).then_inc(ones_ready, 1)
            caches = [a[n][0].rearrange("n (u s) c h d -> (n u) (s c h d)", s=CH) for n in ("cache_cmp_kv", "cache_sel_kv")]

            def gather(dst, which, b, s):
                pool.indirect_dma_start(dst[:].rearrange("p s e -> p (s e)"), None, caches[which],
                                        bass.IndirectOffsetOnAxis(idx[:, b:b + 1], 0)).then_inc(s, 16)

            def lo(u, i=None, per=0):
                n, half = load_of(u)
                k, c = phase_of(u), cols(u)
                pool.wait_ge(hi_done, u + 1 if i is None else i * per + (u + 1))
                w = u % WS
                pool.tensor_tensor(tile(wlo, w, k, u), raw_tile(u), tile(whi, w, k, u).bitcast(F32), ALU.subtract)\
                    .then_inc(lo_done, 1)

            def cols(u):
                return 24 if u == U_M3 - 1 else P

            def tile(t, w, k, u):
                v = t[:, w, 0:k, 0:cols(u)]
                return v.rearrange("p k (g d) -> p k g d", g=KVH) if U_M1 + 12 <= u < U_M1 + 16 else v

            def raw_tile(u):
                n, half = load_of(u)
                r = raw[n % 2][:, 0:phase_of(u), :]
                if U_M1 + 12 <= u < U_M1 + 16:
                    return r.rearrange("p k (g u d) -> p k g u d", g=KVH, u=2)[:, :, :, half, :]
                return r[:, :, half * P:half * P + cols(u)]

            pool.wait_ge(idx_ready, 1)
            for b in range(2):
                gather(XC[b], 0, b, xc_loaded[b])
            for u in range(4):
                lo(u)
            for b in range(2, DB):
                if b % 2 == 0:
                    pool.wait_ge(xt_a, 8 * (b // 2))
                    pool.wait_ge(xt_d, 8 * (b // 2))
                gather(XC[b % 2], 0, b, xc_loaded[b % 2])

            def ffn_lo(u0):
                for iters in (KA // 2, KB // 2):
                    first = 1 if u0 == 0 else 0
                    with pool.Fori(first, iters) as i:
                        for j in range(4):
                            lo(u0 + j, i, 4)
                    u0 += 4 * iters
                    with pool.Fori(0, 2) as i:
                        for j in range(4):
                            lo(u0 + j, i, 4)
                    u0 += 8

            ffn_lo(U_F1)
            for u in range(U_M1, U_M3):
                lo(u)
            for v in range(2):
                for b in range(DB):
                    if v == 0 and b < 2:
                        pool.wait_ge(cph_done, 2)
                    elif v == 0:
                        pool.wait_ge(tp_done, TB + 5 * (b - 1))
                    elif b < 2:
                        pool.wait_ge(tp_done, TB + 5 * (DB - 1 + b))
                    else:
                        pool.wait_ge(sv_done, b - 1)
                    gather(GB[b % 2], 1, b, gb_loaded[b % 2])
            pool.wait_ge(os_lo, 1)
            with pool.Fori(0, 4) as i:
                for j in range(8):
                    lo(U_M3 + j, i, 8)
            for u in range(U_M4, U_F2):
                lo(u)
            ffn_lo(U_F2)

        @block.scalar
        def _(act):
            def cols(u):
                return 24 if u == U_M3 - 1 else P

            def hi(u, i=None, per=0):
                n, half = load_of(u)
                k = phase_of(u)
                if half == 0:
                    r = raw_count(n)
                    if i is None:
                        act.wait_ge(raw_loaded[n % 2], r)
                    else:
                        step = raw_count(n + per // 2) - r
                        act.wait_ge(raw_loaded[n % 2], i * step + r)
                if u >= WS:
                    g = group(u - WS) + 1
                    act.wait_ge(grp_done, g if i is None else i * per + g)
                dst = whi[:, u % WS, 0:k, 0:cols(u)]
                src = raw[n % 2][:, 0:k, :]
                if U_M1 + 12 <= u < U_M1 + 16:
                    dst = dst.rearrange("p k (g d) -> p k g d", g=KVH)
                    src = src.rearrange("p k (g u d) -> p k g u d", g=KVH, u=2)[:, :, :, half, :]
                else:
                    src = src[:, :, half * P:half * P + cols(u)]
                act.activation(dst, src, ACT.Copy).then_inc(hi_done, 1)

            act.wait_ge(ident_loaded, 16)
            act.activation(bump[:, 0:1], ident[:, 0:1], ACT.Copy).then_inc(xt_ev_a, 2)
            act.wait_ge(pe_tp, 1)
            act.activation(pet[:, :, :].rearrange("p k j -> p (k j)"), bank[:, 4, 0:32], ACT.Copy).then_inc(pe_ev, 1)
            act.activation(sc[:, :, :, :].rearrange("p c k b -> p k c b"),
                           bank[:, 4, 64:128].rearrange("p (k c b) -> p k c b", k=2, c=4), ACT.Copy).then_inc(sc_ready, 1)
            act.wait_ge(hpe_done, 1)
            act.activation(hpe[:, :], bank[:, 5, 0:2], ACT.Copy).then_inc(hpe_ready, 1)
            for u in range(4):
                hi(u)
            with act.Fori(0, DB // 2) as i:
                for kk in range(2):
                    for s in range(0, 8, 2):
                        n = 4 * kk + s // 2
                        act.wait_ge(xt_a, i * 8 + (n + 1))
                        if s == 0:
                            act.wait_ge(hid_done, i * 2 + (kk + 1))
                        for dst, src in halves(XT[kk], s, (s // 2 % 2) * 2):
                            ins = act.activation(dst, src, ACT.Copy)
                        ins.then_inc(xt_ev_a, 1)
                for kk in range(2):
                    act.wait_ge(hid_done, i * 2 + (kk + 3))
                    act.wait_ge(cmp_done, i * 2 + (kk + 1))
                    act.activation(SH[kk][:, :, :].rearrange("p a c -> p (a c)"), bank[:, 4 + kk, 0:4 * NCMP], ACT.Silu,
                                   bias=hpe[:, kk:kk + 1]).then_inc(hid_act, 1)

            def split_x(k, c):
                act.activation(xh[:, c, :], xT[:, c, :], ACT.Copy, scale=gn4[:, k, c:c + 1]).then_inc(xh_done, 1)

            act.wait_ge(const_loaded, 16 * 16)
            for c in range(DC):
                act.wait_ge(acc_free, G_X + c + 1)
                split_x(0, c)

            def root(k):
                act.wait_ge(acc_free, G_ST[k] + 1)
                act.activation(tmp[5][:, :], tmp[5][:, :], ACT.Sqrt).then_inc(std_ready, 1)

            def ffn(u0, nk, h0):
                for half, iters in enumerate((KA // 2, KB // 2)):
                    def body(i, last):
                        for j in range(4):
                            u = u0 + j
                            if last:
                                hi(u + 4 * iters)
                            else:
                                hi(u + 4, i, 4)
                            e = (iters - 1) * 4 if last else i * 4
                            e2 = (iters - 1) * 2 if last else i * 2
                            if j < 2:
                                act.wait_ge(acc_free, e + (group(u) + 1))
                                act.activation(tmp[j][:, :], tmp[j][:, :], ACT.Silu).then_inc(silu_done, 1)
                            else:
                                act.wait_ge(h_ready, e2 + (h0 + j - 1))
                                c = (iters - 1) * 2 + j - 2 if last else i * 2 + (j - 2)
                                dst = hh[:, c, :] if last else hh[:, bass.ds(c, 1), :].rearrange("p o t -> p (o t)")
                                act.activation(dst, tmp[1 + j][:, :], ACT.Copy).then_inc(hh_done, 1)
                    with act.Fori(0, iters - 1) as i:
                        body(i, False)
                    body(None, True)
                    u0 += 4 * iters
                    h0 += 2 * iters
                    for d in range(DC):
                        if u0 + d + 4 < U_END:
                            hi(u0 + d + 4)
                        if half == 1 and nk is not None:
                            act.wait_ge(acc_free, group(u0 + d) + 1)
                            split_x(nk, d)
                    u0 += DC

            root(0)
            ffn(U_F1, 1, 0)
            root(1)
            for t in range(23):
                if U_M1 + t + 4 < U_M3:
                    hi(U_M1 + t + 4)
                if 8 <= t < 12:
                    c = t - 8
                    act.wait_ge(v_ready, c + 1)
                    act.activation(vch[:, c, :], tmp[2 + c % 2][:, :], ACT.Copy).then_inc(vch_done, 1)
            act.wait_ge(acc_free, group(U_M3 - 1) + 1)
            act.activation(gnT[:, :], gnT[:, :], ACT.Sigmoid).then_inc(gn_sig, 1)
            for t in range(QT):
                act.wait_ge(tp_done, t + 1)
                act.activation(rows[:, t, :], bank[:, 2 * t:2 * t + 2, :].rearrange("p a b -> p (a b)")[:, 0:3 * ROW], ACT.Copy)\
                    .then_inc(tp_ev, 1)
            act.wait_ge(tp_done, 5)
            act.activation(srows[:, :], bank[0:DB, 0:2, :].rearrange("p a b -> p (a b)")[:, 0:3 * ROW], ACT.Copy).then_inc(tp_ev, 1)
            act.wait_ge(tp_done, 6)
            act.activation(trow[:, :], bank[0:10, 2, :], ACT.Copy).then_inc(tp_ev, 1)
            act.wait_ge(tp_done, 7)
            act.activation(gt[:, :, :].rearrange("p t e -> p (t e)"), bank[:, 3, 0:96], ACT.Copy).then_inc(gt_ready, 1)
            act.activation(gts[:, :], bank[0:DB, 3, 96:120], ACT.Copy).then_inc(tp_ev, 1)
            act.wait_ge(sc_nm, 1)
            act.activation(ps[:, PAST + 1 + SEQ:PAST + 1 + SEQ + NCMP], scs[:, 0:NCMP], ACT.Exp, bias=sst[:, 1:2], scale=SCALE,
                           accum_out=sst[:, 2:3]).then_inc(sc_exp, 1)
            for kk in range(2):
                act.wait_ge(tp_done, 8 + kk)
                for r in range(2):
                    for g in range(KVH):
                        src = bank[HD * g:HD * (g + 1), (4, 0)[kk], :].rearrange("p (s r c) -> p s r c", r=2, c=PCH)[:, :, r, :]
                        ins = act.activation(xtp[kk][HD * r:HD * (r + 1), :, g, :], src, ACT.Copy)
                ins.then_inc(tp_ev, 1)
            for kk in range(2):
                act.wait_ge(cph_done, kk + 1)
                act.activation(shp[kk][:, :], bank[:, 6 + kk, 0:KVH * PCMP], ACT.Silu, bias=hpe[:, kk:kk + 1]).then_inc(cph_act, 1)
            act.wait_ge(cpo_done, 1)
            act.activation(kcP[:, :], bank[:, 4, 0:PCMP], ACT.Copy).then_inc(cpo_ev, 1)
            act.wait_ge(cpo_done, 2)
            act.activation(vcP[:, :], bank[0:PCMP, 0, 0:P], ACT.Copy).then_inc(cpo_ev, 1)
            with act.Fori(0, DB // 2) as i:
                for q in range(10):
                    act.wait_ge(tp_done, i * 10 + (TB + q + 1))
                    act.wait_ge(kt_used, i * 10 + (q + 1))
                    act.activation(kt[q % 2][:, :], bank[:, 6 + q % 2, :], ACT.Copy).then_inc(tp_ev, 1)
            act.wait_ge(snm, 1)
            act.activation(ps[:, 0:PAST + 1], ps[:, 0:PAST + 1], ACT.Exp, bias=sst[:, 5:6], scale=SCALE,
                           accum_out=sst[:, 6:7]).then_inc(sexp, 1)
            act.wait_ge(snm, 2)
            act.activation(ps[:, PAST + 1:PAST + 1 + SEQ], bank[0:64, 4, :], ACT.Exp, bias=sst[:, 9:10], scale=SCALE,
                           accum_out=sst[:, 10:11]).then_inc(sexp, 1)

            for n, m in enumerate((8, 8, 5)):
                act.wait_ge(tp_done, TBS + n + 1)
                act.activation(pst[:, 8 * n:8 * n + m, :].rearrange("p s e -> p (s e)"), bank[:, n, 0:64 * m], ACT.Copy).then_inc(tp_ev, 1)

            def empty(b, j, nxt=0):
                t = [0, 1, 5, 9, 10, 14][b] + 18 * nxt
                if b:
                    act.wait_ge(pv_done, j * 6 + b)
                if b % 3 == 0:
                    act.wait_ge(tp_done, j * 18 + (TBP + t + 1))
                    act.activation(ptc[:, :], bank[0:PCMP, 4 + t % 2, :], ACT.Copy).then_inc(tp_ev, 1)
                    return
                for q in range(QT):
                    act.wait_ge(tp_done, j * 18 + (TBP + t + q + 1))
                    act.activation(ptp[:, 0:q + 1, q * P:(q + 1) * P],
                                   bank[:, 4 + (t + q) % 2, 0:(q + 1) * P].rearrange("p (k n) -> p k n", n=P), ACT.Copy)\
                        .then_inc(tp_ev, 1)

            def exps(b, j, nxt=0):
                if b % 3 == 0:
                    act.wait_ge(cmp_nm, j * 2 + (2 * nxt + b // 3 + 1))
                    act.activation(cm[b // 3][:], cm[b // 3][:], ACT.Exp, scale=SCALE).then_inc(cmp_exp, 1)
                    return
                n = b - 1 - b // 3
                act.wait_ge(big_nm, j * 4 + (4 * nxt + n + 1))
                for q in range(QT):
                    v = sm[n % 2][:, q * (q + 1) // 2 * P:(q + 1) * (q + 2) // 2 * P]
                    act.activation(v, v, ACT.Exp, bias=nmx[:, n % 2, q:q + 1], scale=SCALE,
                                   accum_out=lsm[:, n % 2, q:q + 1]).then_inc(big_exp, 1)

            def attend(j, last):
                for b in range(1, 5):
                    exps(b + 1, j)
                    empty(b, j)
                if not last:
                    exps(0, j, 1)
                empty(5, j)
                if not last:
                    exps(1, j, 1)
                act.wait_ge(pv_done, j * 6 + 6)
                act.activation(oth[:, bass.ds(j, 1), 0:SEQ].rearrange("p o t -> p (o t)"), bank[:, 6, :], ACT.Copy)\
                    .then_inc(o_hi, 1)
                if not last:
                    empty(0, j, 1)

            exps(0, 0)
            exps(1, 0)
            empty(0, 0)
            with act.Fori(0, HPG - 1) as j:
                attend(j, False)
            attend(HPG - 1, True)
            act.wait_ge(o64_ready, 2)
            act.activation(oth[:, :, SEQ:T].rearrange("p j b -> p b j"), oS[:, :].rearrange("p (b j) -> p b j", j=4), ACT.Copy)\
                .then_inc(os_hi, 1)
            for u in range(4):
                hi(U_M3 + u)

            def m3(i):
                for k in range(8):
                    u = U_M3 + k
                    if i is not None:
                        hi(u + 4, i, 8)
                    else:
                        hi(u + 4 + 24 if k < 4 else U_M4 + k - 4)
                    if k < 4:
                        act.wait_ge(acc_free, (24 if i is None else i * 8) + (group(u) + 1))
                        act.activation(tmp[k][:, :], tmp[k][:, :], ACT.Sigmoid).then_inc(sig_done, 1)

            with act.Fori(0, 3) as i:
                m3(i)
            m3(None)
            act.wait_ge(grp_done, group(U_M4 - 1) + 1)
            for d in range(DC):
                act.wait_ge(m_ready, d + 1)
                act.activation(mh[:, d, :], mm[:, d, :], ACT.Copy).then_inc(mh_done, 1)
            for d in range(DC):
                hi(U_M4 + 4 + d)
                act.wait_ge(acc_free, group(U_M4 + d) + 1)
                split_x(2, d)
            root(2)
            ffn(U_F2, None, DFC)
            act.wait_ge(fms_ready, 1)
            act.activation(st5[:, :], st5[:, :], ACT.Sqrt).then_inc(fstd_ready, 1)
            act.wait_ge(fr_ready, 1)
            for t in range(QT + 1):
                p = P if t < QT else DB
                act.wait_ge(y_tp, t + 1)
                act.activation(yr[t][0:p, :], bank[0:p, 2 * (t % 4):2 * (t % 4) + 2, :].rearrange("p a b -> p (a b)"), ACT.Copy,
                               scale=st5[0:p, t:t + 1]).then_inc(y_ev, 1)

        @block.vector
        def _(dve):
            tt, ts, stt = dve.tensor_tensor, dve.tensor_scalar, dve.scalar_tensor_tensor
            dve.memset(bump[:, 1:2], 0.0).then_inc(xt_ev_d, 2)
            dve.memset(bump[:, 2:3], 0.0).then_inc(cmp_ev, 2)
            dve.wait_ge(ptab_loaded, 16 * 9)
            ts(idx[:, :], ptab[:, :], 8.0, sub[:, 0:1], ALU.mult, ALU.add).then_inc(idx_ready, 1)
            with dve.Fori(0, DB // 2) as i:
                for kk in range(2):
                    for s in range(1, 8, 2):
                        n = 4 * kk + s // 2
                        dve.wait_ge(xt_d, i * 8 + (n + 1))
                        if s == 1:
                            dve.wait_ge(hid_done, i * 2 + (kk + 1))
                        for dst, src in halves(XT[kk], s, (s // 2 % 2) * 2 + 1):
                            ins = dve.tensor_copy(dst, src)
                        ins.then_inc(xt_ev_d, 1)
                dve.wait_ge(cmp_done, i * 2 + 3)
                dve.tensor_copy(kcS[:, bass.ds(i * 2, 2), :], bank[:, 6, 0:2 * NCMP].rearrange("p (b c) -> p b c", b=2)).then_inc(cmp_ev, 1)
                dve.wait_ge(cmp_done, i * 2 + 4)
                dve.tensor_copy(vcS[:, bass.ds(i * 2, 2), :], bank[0:NCMP, 7, 0:2 * P].rearrange("p (b c) -> p b c", b=2)).then_inc(cmp_ev, 1)

            xs = Steps(dve, x_step)
            XL = (0, DC, 2 * DC)

            def prep(k, c):
                dst = ssq if c == 0 else tmp[6]
                ins = tt(dst[:, :], xT[:, c, :], xT[:, c, :], ALU.mult)
                if c:
                    xs.did(ins)
                    xs.wait()
                    ins = tt(ssq[:, :], ssq[:, :], tmp[6][:, :], ALU.add)
                if c == DC - 1:
                    ins.then_inc(ssq_ready, 1)
                else:
                    xs.did(ins)
                if k < 3:
                    dve.wait_ge(xh_done, XL[k] + c + 1)
                    stt(xl[:, c, :], xT[:, c, :], gn4[:, k, c:c + 1], xh[:, c, :].bitcast(F32), ALU.mult, ALU.subtract)\
                        .then_inc(xl_done, 1)
                else:
                    ts(xg[:, c, :], xT[:, c, :], gn4[:, k, c:c + 1], None, ALU.mult).then_inc(xg_ready, 1)
                if c < DC - 1:
                    xs.wait()

            def stats(k):
                g = G_ST[k]
                dve.wait_ge(grp_done, g + 1)
                ts(two(tmp[5][:, :]), acc(g), 1.0 / D, EPS, ALU.mult, ALU.add).then_inc(acc_free, 1)
                dve.wait_ge(std_ready, k + 1)
                dve.reciprocal(rr[:, :], tmp[5][:, :]).then_inc(r_ready, 1)
                dve.wait_ge(r_ready, k + 1)

            for c in range(DC):
                dve.wait_ge(grp_done, G_X + c + 1)
                dve.tensor_copy(xT[:, c, :], flat(c, T)).then_inc(acc_free, 1)
                dve.wait_ge(acc_free, G_X + c + 1)
                prep(0, c)
            stats(0)

            def ffn(u0, nk, h0):
                for half, iters in enumerate((KA // 2, KB // 2)):
                    with dve.Fori(0, iters) as i:
                        for j in range(4):
                            g = group(u0 + j)
                            dve.wait_ge(grp_done, i * 4 + (g + 1))
                            dst = tmp[j] if j < 2 else tmp[2]
                            tt(two(dst[:, :]), acc(g), two(rr[:, :]), ALU.mult).then_inc(acc_free, 1)
                            if j >= 2:
                                dve.wait_ge(acc_free, i * 4 + (g + 1))
                                dve.wait_ge(silu_done, i * 2 + (h0 + j - 1))
                                tt(tmp[1 + j][:, :], tmp[j - 2][:, :], tmp[2][:, :], ALU.mult).then_inc(h_ready, 1)
                                dve.wait_ge(hh_done, i * 2 + (h0 + j - 1))
                                c = bass.ds(i * 2 + (j - 2), 1)
                                tt(hl[:, c, :].rearrange("p o t -> p (o t)"), tmp[1 + j][:, :],
                                   hh[:, c, :].rearrange("p o t -> p (o t)").bitcast(F32), ALU.subtract).then_inc(hl_done, 1)
                    u0 += 4 * iters
                    h0 += 2 * iters
                    for d in range(DC):
                        g = group(u0 + d)
                        dve.wait_ge(grp_done, g + 1)
                        stt(two(xT[:, d, :]), acc(g), 0.5, two(xT[:, d, :]), ALU.mult, ALU.add).then_inc(acc_free, 1)
                        if half == 1:
                            dve.wait_ge(acc_free, g + 1)
                            prep(nk, d)
                    u0 += DC

            ffn(U_F1, 1, 0)
            stats(1)

            ms = Steps(dve, m_step)
            for k in range(2):
                ms.did(tt(cs[:, k, :], cs[:, k, :], rr[:, :], ALU.mult))
            ms.wait()

            def scaled(dst, t, p=P):
                g = group(U_M1 + t)
                dve.wait_ge(grp_done, g + 1)
                tt(two(dst), acc(g)[0:p], two(rr[0:p, :]), ALU.mult).then_inc(acc_free, 1)
                return g + 1

            def rope(dst, t):
                g = group(U_M1 + t)
                dve.wait_ge(grp_done, g + 1)
                ms.wait()
                ms.did(tt(two(tmp[4][:, :]), acc(g), two(cs[:, 0, :]), ALU.mult))
                for q in range(4):
                    s, d = slice(32 * q, 32 * q + 32), slice(32 * (q ^ 1), 32 * (q ^ 1) + 32)
                    ins = tt(two(tmp[5][d, :]), acc(g)[s], two(cs[s, 1, :]), ALU.mult)
                    if q < 3:
                        ms.did(ins)
                ins.then_inc(acc_free, 1)
                dve.wait_ge(acc_free, g + 1)
                ms.wait()
                ms.did(tt(dst, tmp[4][:, :], tmp[5][:, :], ALU.add))

            dve.wait_ge(sc_ready, 1)
            for t in range(4):
                scaled(ub[:, t, :], t)
            for t in range(4, 8):
                scaled(ui[:, t - 4, :], t)
            for c in range(4):
                dve.wait_ge(acc_free, scaled(tmp[0][:, :], 8 + c))
                u, y, v = ui[:, c, :], tmp[1], tmp[2 + c % 2]

                def tap(k):
                    return cw[:, k, c:c + 1]

                ms.did(tt(u, tmp[0][:, :], u, ALU.mult))
                ms.wait()
                ms.did(dve.tensor_copy(tail[:, c, :], u[:, SEQ - 2:T]))
                ms.did(ts(y[:, :], u, tap(2), None, ALU.mult))
                ms.wait()
                ms.did(stt(y[:, 2:SEQ], u[:, 0:SEQ - 2], tap(0), y[:, 2:SEQ], ALU.mult, ALU.add))
                ms.did(stt(y[:, SEQ:T], sc[:, c, 0, :], tap(0), y[:, SEQ:T], ALU.mult, ALU.add))
                ms.wait()
                ms.did(stt(y[:, 1:SEQ], u[:, 0:SEQ - 1], tap(1), y[:, 1:SEQ], ALU.mult, ALU.add))
                ms.did(stt(y[:, SEQ:T], sc[:, c, 1, :], tap(1), y[:, SEQ:T], ALU.mult, ALU.add))
                ms.wait()
                tt(v[:, :], y[:, :], ub[:, c, :], ALU.mult).then_inc(v_ready, 1)
                dve.wait_ge(vch_done, c + 1)
                tt(vcl[:, c, :], v[:, :], vch[:, c, :].bitcast(F32), ALU.subtract).then_inc(vcl_done, 1)
            for j in range(4):
                rope(Q[:, j, :], 12 + j)
            for t in range(3):
                rope(kv[:, 3 + t, :], 16 + 2 * t)
                scaled(kv[:, t, :], 17 + 2 * t)
            scaled(gnT[:, :], 22, 24)
            dve.wait_ge(acc_free, group(U_M3 - 1) + 1)
            ms.wait()
            dve.memset(bump[:, 3:4], 0.0).then_inc(kv_ready, 1)

            st = Steps(dve, s_step)
            dve.wait_ge(tp_done, 7)
            st.did(dve.memset(qp[:, :, :], 0.0))
            dve.memset(zz[:, :], 0.0).then_inc(zz_ready, 1)
            st.wait()
            for g in range(KVH):
                ins = dve.tensor_copy(qp[HD * g:HD * (g + 1), :, HPG * g:HPG * (g + 1)],
                                      Q[HD * g:HD * (g + 1), :, SEQ:T].rearrange("p j b -> p b j"))
            ins.then_inc(qp_ready, 1)
            dve.wait_ge(scm_done, 1)
            dve.tensor_copy(scs[:, 0:P + 1], bank[0:64, 5, 0:P + 1]).then_inc(scs_ready, 1)
            dve.wait_ge(scs_ready, 1)

            def neg_max(src, c, s, v):
                st.did(dve.tensor_reduce(sst[:, c:c + 1], src, AX.X, ALU.max, negate=True))
                st.wait()
                ts(sst[:, c + 1:c + 2], sst[:, c:c + 1], SCALE, None, ALU.mult).then_inc(s, 1)

            neg_max(scs[:, 0:NCMP], 0, sc_nm, 1)
            dve.wait_ge(sc_exp, 1)
            st.did(dve.reciprocal(sst[:, 3:4], sst[:, 2:3]))
            st.wait()
            pcmp = ps[:, PAST + 1 + SEQ:PAST + 1 + SEQ + NCMP]
            ts(pcmp, pcmp, sst[:, 3:4], None, ALU.mult).then_inc(pcn_ready, 1)
            dve.wait_ge(pct_done, 1)
            dve.tensor_reduce(pcS[:, :], bank[0:NCMP, 5, 0:64].rearrange("p (a h) -> p a h", h=HPG), AX.X, ALU.add)\
                .then_inc(pcs_ready, 1)
            dve.wait_ge(imp_done, 1)
            st.did(dve.tensor_copy(scr16[:, :], bank[0:16, 5, 0:NSEL]))
            st.wait()
            st.did(dve.memset(scr16[:, 0:1], BIG))
            st.did(dve.memset(scr16[:, NSEL - 2:NSEL], BIG))
            st.wait()
            s_i = scr16[:, :].unsqueeze(1).to_broadcast([16, NSEL, NSEL])
            s_j = scr16[:, :].unsqueeze(2).to_broadcast([16, NSEL, NSEL])
            dve.wait_ge(tie_loaded, 16)
            st.did(tt(cmp3[:], s_i, s_j, ALU.is_gt))
            st.did(tt(eq3[:], s_i, s_j, ALU.is_equal))
            st.wait()
            st.did(tt(eq3[:], eq3[:], tie3[:], ALU.mult))
            st.wait()
            st.did(tt(cmp3[:], cmp3[:], eq3[:], ALU.add))
            st.wait()
            st.did(dve.tensor_reduce(rk16[:, :], cmp3[:], AX.X, ALU.add))
            st.wait()
            st.did(ts(rk16[:, :], rk16[:, :], float(TOP), 1.0, ALU.is_lt, ALU.subtract))
            st.wait()
            ts(rk16[:, :], rk16[:, :], -NEG, None, ALU.mult).then_inc(selb_ready, 1)
            for b in range(DB):
                if b >= 2:
                    dve.wait_ge(kt_used, 2 + 5 * (b - 1))
                dve.tensor_copy(qps[b % 2][:, :], qp[:, :, :].rearrange("p b c -> p (b c)")[:, 64 * b:64 * b + 64]).then_inc(qps_ready, 1)
            dve.wait_ge(gt_ready, 1)
            g0 = gt[:, :, :].rearrange("p t (h c) -> p t h c", c=3)[:, :, :, 0]
            st.did(tt(g0, g0, valid[:, :].unsqueeze(2).to_broadcast([P, QT, NH]), ALU.mult))
            dve.wait_ge(selx_done, 1)
            st.did(dve.tensor_copy(sb64[:, :], bank[0:64, 5, 0:NSEL]))
            st.wait()
            st.did(tt(ps[:, 0:PAST].rearrange("p (s k c) -> p s k c", s=CH, c=4),
                      bank[0:64, 0:4, :].rearrange("p a b -> p (a b)").rearrange("p (s k c) -> p s k c", s=CH, c=4),
                      sb64[:, 0:NSEL - 1].unsqueeze(1).unsqueeze(3).to_broadcast([64, CH, NSEL - 1, 4]), ALU.add))
            st.did(dve.tensor_copy(ps[:, PAST:PAST + 1], scs[:, P:P + 1]))
            st.wait()
            neg_max(ps[:, 0:PAST + 1], 4, snm, 1)
            neg_max(bank[0:64, 4, :], 8, snm, 2)
            dve.wait_ge(g64_loaded, 16)
            dve.wait_ge(sexp, 2)
            for k, (lo_, n) in enumerate(((0, PAST + 1), (PAST + 1, SEQ))):
                l, f = sst[:, 6 + 4 * k:7 + 4 * k], sst[:, 12 + k:13 + k]
                st.did(dve.reciprocal(f, l))
                st.wait()
                st.did(tt(f, f, g64[:, 1 + k:2 + k], ALU.mult))
                st.wait()
                v = ps[:, lo_:lo_ + n]
                st.did(ts(v, v, f, None, ALU.mult))
            ts(pcmp, pcmp, g64[:, 0:1], None, ALU.mult).then_inc(ps_ready, 1)
            dve.memset(qz[:, :, :], 0.0).then_inc(o_lo, 1)
            dve.wait_ge(o_lo, 1)

            pp = Steps(dve, p_step)

            def stage1(b, j, nxt=0):
                if b % 3 == 0:
                    g = b // 3
                    dve.wait_ge(cmp_s, j * 2 + (2 * nxt + g + 1))
                    dve.wait_ge(tp_done, j * 18 + (18 * nxt + TBP - 18 + 1 + 9 * g))
                    c = cm[g]
                    tt(c[:], bank[:, 7, 0:QT * PCMP].rearrange("p (q n) -> p q n", n=PCMP), cmask[:], ALU.add).then_inc(cmp_rd, 1)
                    dve.wait_ge(cmp_rd, j * 2 + (2 * nxt + g + 1))
                    pp.did(dve.tensor_reduce(cmx[:, g, :], c[:], AX.X, ALU.max))
                    pp.wait()
                    tt(c[:], c[:], cmx[:, g, :].unsqueeze(2).to_broadcast([P, QT, PCMP]), ALU.subtract).then_inc(cmp_nm, 1)
                    return
                n = b - 1 - b // 3
                dve.wait_ge(tp_done, j * 18 + (18 * nxt + TBP + (14 - 18, 18 - 18, 5, 9)[n]))
                dve.wait_ge(big_s, j * 16 + (16 * nxt + 4 * n + 4))
                dve.memset(bump[:, 0:1], 0.0)
                for q in range(QT):
                    dve.tensor_tensor_reduce(sm[n % 2][:, q * (q + 1) // 2 * P:(q + 1) * (q + 2) // 2 * P],
                                             bank[:, q, 0:(q + 1) * P], tri[:, SEQ - (q + 1) * P:SEQ], 1.0, -3e38,
                                             ALU.add, ALU.max, nmx[:, n % 2, q:q + 1])\
                        .then_inc(big_rd, 1)
                dve.wait_ge(big_rd, j * 16 + (16 * nxt + 4 * n + 4))
                ts(nmx[:, n % 2, :], nmx[:, n % 2, :], -SCALE, None, ALU.mult).then_inc(big_nm, 1)

            def stage2(b, j, nxt=0):
                g = b // 3
                gate = gt[:, :, bass.ds(j * 3 + (3 * nxt + 12 * g + b % 3), 1)].rearrange("p t o -> p (t o)")
                if b % 3 == 0:
                    c = cm[g]
                    dve.wait_ge(cmp_exp, j * 2 + (2 * nxt + g + 1))
                    pp.did(dve.tensor_reduce(cfc[:, g, :], c[:], AX.X, ALU.add))
                    pp.wait()
                    pp.did(dve.reciprocal(cfc[:, g, :], cfc[:, g, :]))
                    pp.wait()
                    pp.did(tt(cfc[:, g, :], cfc[:, g, :], gate, ALU.mult))
                    pp.wait()
                    tt(c[:], c[:], cfc[:, g, :].unsqueeze(2).to_broadcast([P, QT, PCMP]), ALU.mult).then_inc(cmp_p, 1)
                    return
                n = b - 1 - g
                dve.wait_ge(big_exp, j * 16 + (16 * nxt + 4 * n + 4))
                pp.did(dve.reciprocal(fct[:, n % 2, :], lsm[:, n % 2, :]))
                pp.wait()
                pp.did(tt(fct[:, n % 2, :], fct[:, n % 2, :], gate, ALU.mult))
                pp.wait()
                for q in range(QT):
                    v = sm[n % 2][:, q * (q + 1) // 2 * P:(q + 1) * (q + 2) // 2 * P]
                    ts(v, v, fct[:, n % 2, q:q + 1], None, ALU.mult).then_inc(big_p, 1)

            def queries(j, nxt=0):
                for g in range(KVH):
                    ins = dve.tensor_copy(qz[HD * g:HD * (g + 1), g, :],
                                          Q[HD * g:HD * (g + 1), bass.ds(j + nxt, 1), 0:SEQ].rearrange("p o t -> p (o t)"))
                ins.then_inc(qz_ready, 1)

            def sampled(j, s):
                dve.wait_ge(sv_done, j * 2 + (s + 1))
                tt(om[:, bass.ds(j * 2 + s, 1), :].rearrange("p o (g d) -> p (o g) d", g=KVH),
                   bank[0:64, 7, 2 * P:3 * P].rearrange("p (g d) -> p g d", g=KVH),
                   dmask[:, bass.ds(j * 4 + 2 * s, 2)].unsqueeze(2).to_broadcast([64, KVH, HD]), ALU.mult).then_inc(sv_rd, 1)

            def attend(j, last):
                if not last:
                    pp.loop(j, 16)
                for b in range(1, 6):
                    if b < 5:
                        stage1(b + 1, j)
                    elif not last:
                        stage1(0, j, 1)
                    stage2(b, j)
                    if b in (1, 4):
                        sampled(j, b // 3)
                    if b == 4 and not last:
                        dve.wait_ge(big_s, j * 16 + 16)
                        queries(j, 1)
                if not last:
                    stage1(1, j, 1)
                    stage2(0, j, 1)
                dve.wait_ge(o_hi, j + 1)
                tt(otl[:, bass.ds(j, 1), 0:SEQ].rearrange("p o t -> p (o t)"), bank[:, 6, :],
                   oth[:, bass.ds(j, 1), 0:SEQ].rearrange("p o t -> p (o t)").bitcast(F32), ALU.subtract).then_inc(o_lo, 1)
                if not last:
                    pp.end(HPG - 1)

            dve.wait_ge(tp_done, TBP)
            dve.memset(bump[:, 0:1], 0.0).then_inc(sv_rd, 1)
            queries(0)
            stage1(0, 0)
            stage1(1, 0)
            stage2(0, 0)
            with dve.Fori(0, HPG - 1) as j:
                attend(j, False)
            attend(HPG - 1, True)

            dve.wait_ge(vn_done, 1)
            dve.wait_ge(sv_rd, 1 + DB)
            st.did(ts(o64b[:, :], bank[0:64, 6, 0:P], ps[:, PAST:PAST + 1], None, ALU.mult))
            st.wait()
            st.did(dve.tensor_reduce(o64[:, :], om[:, :, :].rearrange("p b e -> p e b"), AX.X, ALU.add))
            st.did(tt(o64b[:, :].rearrange("p (g d) -> p g d", g=KVH), o64b[:, :].rearrange("p (g d) -> p g d", g=KVH),
                      gmask[:, :].unsqueeze(2).to_broadcast([64, KVH, HD]), ALU.mult))
            st.wait()
            tt(o64[:, :], o64[:, :], o64b[:, :], ALU.add).then_inc(o64_ready, 1)
            dve.wait_ge(o64_tp, 1)
            st.did(dve.tensor_copy(oT64[:, :], bank[:, 7, 0:64]))
            st.wait()
            pair = oT64[:, :].rearrange("p (b g j) -> p b g j", b=DB, g=KVH)
            tt(oS[:, :].rearrange("p (b j) -> p b j", j=HPG), pair[:, :, 0, :], pair[:, :, 1, :], ALU.add).then_inc(o64_ready, 1)
            dve.wait_ge(os_hi, 1)
            tt(otl[:, :, SEQ:T].rearrange("p j b -> p b j"), oS[:, :].rearrange("p (b j) -> p b j", j=HPG),
               oth[:, :, SEQ:T].rearrange("p j b -> p b j").bitcast(F32), ALU.subtract).then_inc(os_lo, 1)

            with dve.Fori(0, 4) as i:
                for k in range(8):
                    g = group(U_M3 + k)
                    dve.wait_ge(grp_done, i * 8 + (g + 1))
                    if k < 4:
                        tt(two(tmp[k][:, :]), acc(g), two(rr[:, :]), ALU.mult).then_inc(acc_free, 1)
                        continue
                    dve.wait_ge(sig_done, i * 4 + (k - 3))
                    if k < 6:
                        tt(two(tmp[k - 4][:, :]), acc(g), two(tmp[k - 4][:, :]), ALU.mult).then_inc(acc_free, 1)
                    else:
                        tt(two(tmp[k - 2][:, :]), acc(g), two(tmp[k - 4][:, :]), ALU.mult).then_inc(acc_free, 1)
                        dve.wait_ge(acc_free, i * 8 + (g + 1))
                        tt(mm[:, bass.ds(i * 2 + (k - 6), 1), :].rearrange("p o t -> p (o t)"), tmp[k - 6][:, :], tmp[k - 2][:, :],
                           ALU.add).then_inc(m_ready, 1)
                dve.wait_ge(m_ready, i * 2 + 2)
            for d in range(DC):
                dve.wait_ge(mh_done, d + 1)
                tt(ml[:, d, :], mm[:, d, :], mh[:, d, :].bitcast(F32), ALU.subtract).then_inc(ml_done, 1)
            for d in range(DC):
                g = group(U_M4 + d)
                dve.wait_ge(grp_done, g + 1)
                tt(two(xT[:, d, :]), acc(g), two(xT[:, d, :]), ALU.add).then_inc(acc_free, 1)
                dve.wait_ge(acc_free, g + 1)
                prep(2, d)
            stats(2)
            ffn(U_F2, 3, DFC)
            dve.wait_ge(fst_done, 1)
            ts(st5[:, :], bank[:, 0, 0:5], 1.0 / D, EPS, ALU.mult, ALU.add).then_inc(fms_ready, 1)
            dve.wait_ge(fstd_ready, 1)
            dve.reciprocal(st5[:, :], st5[:, :]).then_inc(fr_ready, 1)

        @block.tensor
        def _(pe):
            def turn(dst, src):
                n = src.shape[0]
                return pe.transpose(dst, src, ident[0:n, 0:n])

            pe.wait_ge(cmpw_loaded, 16 * 7)
            pe.wait_ge(ident_loaded, 16)
            for k in range(2):
                turn(bank[:, 4, 16 * k:16 * k + 16], per[:, k, :])
            for k in range(8):
                ins = turn(bank[:, 4, 64 + 8 * k:72 + 8 * k], scr[:, k * P:(k + 1) * P])
            ins.then_inc(pe_tp, 1)
            pe.wait_ge(pe_ev, 1)
            for k in range(2):
                for j in range(16):
                    ins = pe.matmul(bank[:, 5, k:k + 1], w1[:, k, j, :], pet[:, k, j:j + 1], start=(j == 0), stop=(j == 15))
            ins.then_inc(hpe_done, 1)
            pe.wait_ge(sc_ready, 1)
            pe.wait_ge(hpe_ready, 1)
            pe.matmul(bank[:, 6, 0:2], ident[:, :], ident[:, 0:2], start=True, stop=True).then_inc(hid_done, 2)
            pe.matmul(bank[:, 7, 0:2], ident[:, :], ident[:, 0:2], start=True, stop=True).then_inc(cmp_done, 2)
            with pe.Fori(0, DB // 2) as i:
                for b in range(2):
                    pe.wait_ge(xc_loaded[b], i * 16 + 16)
                for kk in range(2):
                    for s in range(8):
                        n = 4 * kk + s // 2
                        pe.wait_ge(xt_ev_d if s % 2 else xt_ev_a, i * 8 + (n + 1))
                        bk = (s // 2 % 2) * 2 + s % 2
                        for r in range(2):
                            for b in range(2):
                                ins = turn(bank[:, bk, (2 * r + b) * P:(2 * r + b + 1) * P],
                                           XC[b][:, 4 * (s // 2) + s % 2 + 2 * r, kk * P:(kk + 1) * P])
                        ins.then_inc(xt_d if s % 2 else xt_a, 1)
                for kk in range(2):
                    pe.wait_ge(xt_ev_a, i * 8 + (4 * kk + 6))
                    pe.wait_ge(xt_ev_d, i * 8 + (4 * kk + 6))
                    for r in range(2):
                        for s in range(8):
                            ins = pe.matmul(bank[:, 4 + kk, 0:4 * NCMP].rearrange("p (a c) -> p a c", a=4), w1[:, kk, 8 * r + s, :],
                                            XT[kk][:, s, :, r:r + NCMP], start=(r + s == 0), stop=(r == 1 and s == 7))
                    ins.then_inc(hid_done, 1)
                for kk in range(2):
                    pe.wait_ge(hid_act, i * 2 + (kk + 1))
                    pe.wait_ge(cmp_ev, i * 2 + (kk + 1))
                    for g in range(KVH):
                        if kk == 0:
                            ins = pe.matmul(bank[HD * g:HD * (g + 1), 6, 0:2 * NCMP].rearrange("p (b c) -> p b c", b=2), w2[:, 0, :],
                                            SH[0][:, :, :].rearrange("p (b g) c -> p b g c", g=KVH)[:, :, g, :], start=True, stop=True)
                        else:
                            for b in range(2):
                                ins = pe.matmul(bank[0:NCMP, 7, b * P + g * HD:b * P + (g + 1) * HD], SH[1][:, 2 * b + g, :], w2[:, 1, :],
                                                start=True, stop=True)
                    ins.then_inc(cmp_done, 1)

            pe.wait_ge(x_loaded, 32)
            pe.wait_ge(cmp_ev, 2 + DB)
            for c in range(DC):
                if c >= WS:
                    pe.wait_ge(acc_free, c - WS + 1)
                v = flat(c, T)
                for t in range(QT):
                    turn(v[:, t * P:(t + 1) * P], xr[:, t, c * P:(c + 1) * P])
                turn(v[:, SEQ:T], xrs[:, c * P:(c + 1) * P]).then_inc(grp_done, 1)

            def stats(k):
                g = G_ST[k]
                pe.wait_ge(ones_ready, 1)
                pe.wait_ge(ssq_ready, k + 1)
                pe.wait_ge(acc_free, g - WS + 1)
                for h in range(2):
                    ins = pe.matmul(acc(g)[:, h, :], ones[:, :], ssq[:, h * HT:(h + 1) * HT], start=True, stop=True)
                ins.then_inc(grp_done, 1)

            def unit(u, xhi, xlo, i=None, per=0, chunk0=0):
                g, k = group(u), phase_of(u)
                m = 24 if u == U_M3 - 1 else P
                pe.wait_ge(lo_done, u + 1 if i is None else i * per + (u + 1))
                pe.wait_ge(acc_free, g - WS + 1 if i is None else i * per + (g - WS + 1))
                for c in range(k):
                    for n, (w, x) in enumerate(((whi, xhi), (whi, xlo), (wlo, xhi))):
                        for h in range(2):
                            ins = pe.matmul(acc(g)[0:m, h, :], w[:, u % WS, c, 0:m], x[:, c, h * HT:(h + 1) * HT],
                                            start=(c == 0 and n == 0), stop=(c == k - 1 and n == 2))
                ins.then_inc(grp_done, 1)

            def ffn(u0, k, h0):
                pe.wait_ge(xl_done, (k + 1) * DC)
                for iters in (KA // 2, KB // 2):
                    with pe.Fori(0, iters) as i:
                        for j in range(4):
                            unit(u0 + j, xh, xl, i, 4)
                    u0 += 4 * iters
                    h0 += 2 * iters
                    pe.wait_ge(hl_done, h0)
                    with pe.Fori(0, 2) as i:
                        for j in range(4):
                            unit(u0 + j, hh, hl, i, 4)
                    u0 += DC

            stats(0)
            ffn(U_F1, 0, 0)
            stats(1)
            pe.wait_ge(xl_done, 2 * DC)
            with pe.Fori(0, 5) as i:
                for j in range(4):
                    unit(U_M1 + j, xh, xl, i, 4)
            for t in range(20, 23):
                unit(U_M1 + t, xh, xl)

            pe.wait_ge(acc_free, group(U_M3 - 1) + 1)
            pe.wait_ge(kv_ready, 1)
            order = (3, 0, 4, 1, 5, 2)

            def rows_of(bk, cols, p):
                v = bank[0:p, bk:bk + 2, :].rearrange("p a b -> p (a b)")
                for e, c in enumerate(order):
                    ins = turn(v[:, e * P:(e + 1) * P], kv[:, c, cols])
                ins.then_inc(tp_done, 1)

            for t in range(QT):
                rows_of(2 * t, slice(t * P, (t + 1) * P), P)
            pe.wait_ge(tp_ev, 1)
            rows_of(0, slice(SEQ, T), DB)
            pe.wait_ge(tp_ev, 2)
            for c in range(4):
                ins = turn(bank[0:10, 2, c * P:(c + 1) * P], tail[:, c, :])
            ins.then_inc(tp_done, 1)
            pe.wait_ge(gn_sig, 1)
            for t in range(QT):
                turn(bank[:, 3, 24 * t:24 * t + 24], gnT[:, t * P:(t + 1) * P])
            turn(bank[0:DB, 3, 96:120], gnT[:, SEQ:T]).then_inc(tp_done, 1)
            pe.wait_ge(qp_ready, 1)
            pe.wait_ge(tp_ev, 3)
            qpf = qp[:, :, :].rearrange("p b c -> p (b c)")
            for b in range(DB):
                pe.matmul(bank[0:64, 5, 0:NCMP], qpf[:, 64 * b:64 * b + 64], kcS[:, b, :], start=(b == 0), stop=(b == DB - 1))
            for b in range(DB):
                ins = pe.matmul(bank[0:64, 5, P:P + 1], qpf[:, 64 * b:64 * b + 64], kv[:, 4, SEQ + b:SEQ + b + 1], start=(b == 0), stop=(b == DB - 1))
            ins.then_inc(scm_done, 1)
            pe.wait_ge(xcp_loaded, 32)
            pe.wait_ge(w1p_loaded, 32)
            for kk in range(2):
                pe.wait_ge(tp_ev, 5 if kk else 3)
                for s in range(CH):
                    ins = turn(bank[:, (4, 0)[kk], s * PCH:(s + 1) * PCH], xcp[:, s, kk * P:(kk + 1) * P])
                ins.then_inc(tp_done, 1)
            for kk in range(2):
                pe.wait_ge(tp_ev, 8 + kk)
                for r in range(2):
                    for s in range(8):
                        ins = pe.matmul(bank[:, 6 + kk, 0:KVH * PCMP].rearrange("p (g c) -> p g c", g=KVH), w1p[:, kk, 8 * r + s, :],
                                        xtp[kk][:, s, :, r:r + PCMP], start=(r + s == 0), stop=(r == 1 and s == 7))
                ins.then_inc(cph_done, 1)
            pe.wait_ge(pcn_ready, 1)
            turn(bank[0:NCMP, 5, 0:64], ps[:, PAST + 1 + SEQ:PAST + 1 + SEQ + NCMP]).then_inc(pct_done, 1)
            pe.wait_ge(cph_act, 1)
            for g in range(KVH):
                ins = pe.matmul(bank[HD * g:HD * (g + 1), 4, 0:PCMP], w2[:, 0, :], shp[0][:, g * PCMP:(g + 1) * PCMP], start=True, stop=True)
            ins.then_inc(cpo_done, 1)
            pe.wait_ge(cph_act, 2)
            for g in range(KVH):
                ins = pe.matmul(bank[0:PCMP, 0, g * HD:(g + 1) * HD], shp[1][:, g * PCMP:(g + 1) * PCMP], w2[:, 1, :], start=True, stop=True)
            ins.then_inc(cpo_done, 1)
            pe.wait_ge(pcs_ready, 1)
            pe.matmul(bank[0:16, 5, 0:NSEL], pcS[:, :], mcs[:, :], start=True, stop=True).then_inc(imp_done, 1)
            pe.wait_ge(cpo_ev, 2)
            pe.wait_ge(zz_ready, 1)
            for k in range(5):
                ins = pe.matmul(bank[0:64, k, :], zz[:, :], tri[:, :], start=True, stop=False)
            ins.then_inc(kt_used, 2)

            def turn_keys(q, i):
                s = q // 5
                if q % 5 == 0:
                    pe.wait_ge(gb_loaded[s], i * 16 + 16)
                if q % 5 == 4:
                    pe.wait_ge(wt_loaded[s], i * 16 + 16)
                pe.wait_ge(tp_ev, i * 10 + (TB + q - 1))
                for t in range(4):
                    src = wt[s][:, t, 0:P] if q % 5 == 4 else GB[s][:, 4 * (q % 5) + t, 0:P]
                    ins = turn(bank[:, 6 + q % 2, t * P:(t + 1) * P], src)
                ins.then_inc(tp_done, 1)

            def score_keys(q, i):
                if q % 5 == 0:
                    pe.wait_ge(qps_ready, i * 2 + (q // 5 + 1))
                pe.wait_ge(tp_ev, i * 10 + (TB + q + 1))
                pe.matmul(bank[0:64, q % 5, :], qps[q // 5][:, :], kt[q % 2][:, :], start=False, stop=False,
                          skip_group_check=True).then_inc(kt_used, 1)

            with pe.Fori(0, DB // 2) as i:
                turn_keys(0, i)
                for q in range(10):
                    if q < 9:
                        turn_keys(q + 1, i)
                    score_keys(q, i)
            for k in range(5):
                pe.matmul(bank[0:64, k, :], zz[:, :], tri[:, :], start=False, stop=True)
            pe.wait_ge(selb_ready, 1)
            pe.matmul(bank[0:64, 5, 0:NSEL], e16[:, :], rk16[:, :], start=True, stop=True).then_inc(selx_done, 1)

            def scores(b, j, nxt=0):
                g = b // 3
                if b % 3 == 0:
                    if g or nxt:
                        pe.wait_ge(cmp_rd, j * 2 + (1 + nxt))
                        pe.wait_ge(sv_rd, j * 2 + (2 + nxt))
                    for q in range(QT):
                        ins = pe.matmul(bank[:, 7, q * PCMP:(q + 1) * PCMP], qz[:, g, q * P:(q + 1) * P], kcP[:, :], start=True, stop=True)
                    ins.then_inc(cmp_s, 1)
                    return
                n = b - 1 - g
                k = kv[:, 3 + b % 3, :]
                for q in range(QT):
                    if n or nxt:
                        pe.wait_ge(big_rd, j * 16 + (16 * nxt + 4 * n - 4 + q + 1))
                    pe.matmul(bank[:, q, 0:(q + 1) * P], qz[:, g, q * P:(q + 1) * P], k[:, 0:(q + 1) * P], start=True, stop=True)\
                        .then_inc(big_s, 1)

            def turns(b, j):
                t = [0, 1, 5, 9, 10, 14][b]
                if b % 3 == 0:
                    pe.wait_ge(cmp_p, j * 2 + (b // 3 + 1))
                    pe.wait_ge(tp_ev, j * 18 + (TBP + t - 1))
                    for q in range(QT):
                        ins = turn(bank[0:PCMP, 4 + t % 2, q * P:(q + 1) * P], cm[b // 3][:, q, :])
                    ins.then_inc(tp_done, 1)
                    return
                n = b - 1 - b // 3
                for q in range(QT):
                    pe.wait_ge(big_p, j * 16 + (4 * n + q + 1))
                    pe.wait_ge(tp_ev, j * 18 + (TBP + t + q - 1))
                    for k in range(q + 1):
                        c = q * (q + 1) // 2 * P + k * P
                        ins = turn(bank[:, 4 + (t + q) % 2, k * P:(k + 1) * P], sm[n % 2][:, c:c + P])
                    ins.then_inc(tp_done, 1)

            def values(b, j):
                g, t = b // 3, [1, 5, 9, 10, 14, 18][b]
                pe.wait_ge(tp_ev, j * 18 + (TBP + t))
                out = bank[HD * g:HD * (g + 1), 6, :]
                if b % 3 == 0:
                    if g == 0:
                        pe.wait_ge(o_lo, j + 1)
                    pe.matmul(out, vcP[:, g * HD:(g + 1) * HD], ptc[:, :], start=True, stop=False).then_inc(pv_done, 1)
                    return
                for k in reversed(range(QT)):
                    c = (b % 3) * ROW + P + g * HD
                    ins = pe.matmul(out[:, k * P:SEQ], rows[:, k, c:c + HD], ptp[:, k, k * P:SEQ], start=False,
                                    stop=(b % 3 == 2 and k == 0))
                ins.then_inc(pv_done, 1)

            def sampled(j, s):
                pe.wait_ge(gb_loaded[s], j * 16 + 16 * 5)
                pe.wait_ge(wt_loaded[s], j * 16 + 16 * 5)
                pe.wait_ge(cmp_rd, j * 2 + (1 + s))
                pe.wait_ge(sv_rd, j * 2 + (s + 1))
                out = bank[0:64, 7, 2 * P:3 * P]
                for t in range(16):
                    pe.matmul(out, pst[:, t, :], GB[s][:, t, P:2 * P], start=(t == 0), stop=False)
                for t in range(4):
                    pe.matmul(out, pst[:, 16 + t, :], wt[s][:, t, P:2 * P], start=False, stop=False)
                pe.matmul(out, pst[0:NCMP, 20, :], vcS[:, bass.ds(j * 2 + s, 1), :].rearrange("p o e -> p (o e)"),
                          start=False, stop=True).then_inc(sv_done, 1)

            def attend(j, last):
                for b in range(6):
                    turns(b, j)
                    if b < 4:
                        scores(b + 2, j)
                    elif not last:
                        if b == 4:
                            pe.wait_ge(qz_ready, j + 2)
                        scores(b - 4, j, 1)
                    values(b, j)
                    if b % 3 == 0:
                        sampled(j, b // 3)

            pe.wait_ge(ps_ready, 1)
            for n, m in enumerate((8, 8, 5)):
                for s in range(8 * n, 8 * n + m):
                    c = s * P if s < 16 else PAST + 1 + (s - 16) * P
                    w = P if s < 20 else NCMP
                    ins = turn(bank[0:w, n, (s - 8 * n) * 64:(s - 8 * n + 1) * 64], ps[:, c:c + w])
                ins.then_inc(tp_done, 1)
            pe.wait_ge(tp_ev, TBP)
            pe.wait_ge(qz_ready, 1)
            scores(0, 0)
            scores(1, 0)
            with pe.Fori(0, HPG - 1) as j:
                attend(j, False)
            attend(HPG - 1, True)
            pe.wait_ge(o_lo, 1 + HPG)
            pe.matmul(bank[0:64, 6, 0:P], e8[:, :], srows[:, ROW + P:2 * ROW], start=True, stop=True).then_inc(vn_done, 1)
            pe.wait_ge(o64_ready, 1)
            turn(bank[:, 7, 0:64], o64[:, :]).then_inc(o64_tp, 1)
            pe.wait_ge(os_lo, 1)
            with pe.Fori(0, 4) as i:
                for k in range(8):
                    x = ((xh, xl), (vch, vcl), (oth, otl))[0 if k < 4 else k // 2 - 1]
                    unit(U_M3 + k, *x, i, 8)
            pe.wait_ge(ml_done, DC)
            with pe.Fori(0, 2) as i:
                for j in range(4):
                    unit(U_M4 + j, mh, ml, i, 4)
            stats(2)
            ffn(U_F2, 2, DFC)
            pe.wait_ge(ssq_ready, 4)
            pe.wait_ge(acc_free, group(U_END - 1) + 1)
            pe.matmul(bank[:, 0, QT:QT + 1], ssq[:, 0:P], ones[:, 0:1], start=True, stop=True)
            for t in range(QT + 1):
                p = P if t < QT else DB
                ins = pe.matmul(bank[0:p, 0, t:t + 1], ssq[:, t * P:t * P + p], ones[:, 0:1], start=True, stop=True)
            ins.then_inc(fst_done, 1)
            pe.wait_ge(xg_ready, DC)
            for t in range(QT + 1):
                p = P if t < QT else DB
                if t == 0:
                    pe.wait_ge(fms_ready, 1)
                if t >= 4:
                    pe.wait_ge(y_ev, t - 3)
                v = bank[0:p, 2 * (t % 4):2 * (t % 4) + 2, :].rearrange("p a b -> p (a b)")
                for c in range(DC):
                    ins = turn(v[:, c * P:(c + 1) * P], xg[:, c, t * P:t * P + p])
                ins.then_inc(y_tp, 1)


_KV = (2, KVH, HD)
_OUTS = [('y_prompt', (1, SEQ, D)), ('y_sample', (DB, 1, D)), ('cmp_kv_prompt', (1, 1, SEQ) + _KV), ('sel_kv_prompt', (1, 1, SEQ) + _KV),
         ('win_kv_prompt', (1, 1, SEQ) + _KV), ('conv_prompt', (1, 1, 2, DCV)), ('cmp_kv_sample', (1, DB, 1) + _KV),
         ('sel_kv_sample', (1, DB, 1) + _KV), ('win_kv_sample', (1, DB, SEQ) + _KV), ('conv_sample', (1, DB, 2, DCV))]


def constants():
    f = np.float32
    c = {}
    c["c_ident"] = np.eye(P, dtype=f)
    c["c_sub"] = (np.arange(P) % 8).astype(f)[:, None]
    pos = np.concatenate([np.arange(SEQ), np.full(DB, PAST)]).astype(f)
    freq = np.power(10000.0, -np.arange(HD // 2) * (2.0 / HD)).astype(f)
    ang = (pos[None, :] * freq[:, None]).astype(f)
    cos, sin = np.cos(ang).astype(f), np.sin(ang).astype(f)
    c["c_cs"] = np.stack([np.tile(cos, (4, 1)), np.concatenate([sin, -sin, sin, -sin])], 1)
    q = np.arange(P)
    tri = np.zeros((P, SEQ), f)
    tri[:, SEQ - P:] = np.where(q[None, :] <= q[:, None], 0, NEG)
    c["c_tri"] = tri
    tok = np.arange(QT)[None, :] * P + q[:, None]
    end = np.arange(PCMP) * CH + 2 * CH - 1
    c["c_cmask"] = np.where(end[None, None, :] <= tok[:, :, None], 0, NEG).astype(f)
    c["c_valid"] = (tok >= end[0]).astype(f)
    start = np.arange(NCMP)[:, None] * CH
    jb = np.arange(NSEL)[None, :] * 64
    c["c_mcs"] = ((start < jb + 64) & (start + 2 * CH > jb)).astype(f)
    r = np.arange(64)
    c["c_e16"] = (r[None, :] // HPG == np.arange(16)[:, None]).astype(f)
    c["c_e8"] = (r[None, :] // NH == np.arange(DB)[:, None]).astype(f)
    c["c_dmask"] = (r[:, None] // HPG == np.arange(DB * KVH)[None, :]).astype(f)
    c["c_gmask"] = (r[:, None] // HPG % KVH == np.arange(KVH)[None, :]).astype(f)
    n = np.arange(NSEL)
    c["c_tie"] = np.broadcast_to((n[None, :] < n[:, None]).astype(f), (16, NSEL, NSEL)).copy()
    return c


def kernel(**inputs):
    import numpy as _np
    import concourse.bacc as _bacc
    from concourse import mybir as _mybir
    from concourse.bass_utils import run_bass_kernel_spmd as _run

    nc = _bacc.Bacc("TRN2", target_bir_lowering=False, num_devices=1)
    arrays, aps = {}, {}
    for name, v in list(inputs.items()) + list(constants().items()):
        v = _np.ascontiguousarray(v)
        arrays[name] = v
        aps[name] = nc.dram_tensor(name, v.shape, _mybir.dt.from_np(v.dtype), kind="ExternalInput").ap()
    for name, shape in _OUTS:
        aps[name] = nc.dram_tensor(name, shape, _mybir.dt.float32, kind="ExternalOutput").ap()
    build(nc, aps)
    r = _run(nc, [arrays], core_ids=[0])
    return tuple(r.results[0][name] for name, _ in _OUTS)
```

```python
from contextlib import ExitStack

import numpy as np

import concourse.bass as bass
from concourse import mybir

F32 = mybir.dt.float32
F32R = mybir.dt.float32r
I32 = mybir.dt.int32
U32 = mybir.dt.uint32
ALU = mybir.AluOpType
ACT = mybir.ActivationFunctionType
AX = mybir.AxisListType

P = 128
D = 1024
SEQ = 512
DB = 8
T = SEQ + DB
HT = T // 2
DC = D // P
DFF = 2816
DFC = DFF // P
PAST = 2048
PAGE = 128
CH = 16
NCH = PAST // CH
NCMP = NCH - 1
PCH = SEQ // CH
PCMP = PCH - 1
HD = 64
NH = 8
KVH = 2
HPG = NH // KVH
ROW = 2 * KVH * HD
DCV = 512
NSEL = PAST // 64 + 1
TOP = 16
EPS = 1e-6
BIG = 1e9
NEG = -1e30
SCALE = HD ** -0.5
C_Q = 3 * DCV
C_KV = C_Q + NH * HD
C_GN = C_KV + 3 * ROW
C_GB = C_GN + NH * 3
QT = SEQ // P
WS = 4
KA = 12
KB = DFC - KA

FFN_UNITS = 2 * DFC + 2 * DC
U_F1, U_M1 = 0, FFN_UNITS
U_M3 = U_M1 + 23
U_M4 = U_M3 + 32
U_F2 = U_M4 + 8
U_END = U_F2 + FFN_UNITS
L_F1, L_M1 = 0, FFN_UNITS // 2
L_M3 = L_M1 + 12
L_M4 = L_M3 + 16
L_F2 = L_M4 + 4
G_X = 0
G_ST = [DC, DC + 1 + FFN_UNITS, U_F2 + DC + 2]
OFF_F1, OFF_M, OFF_F2 = DC + 1, DC + 2, DC + 3


def phase_of(u):
    for base in (U_F1, U_F2):
        if base <= u < base + FFN_UNITS:
            v = u - base
            return DC if v < 24 else KA if v < 32 else DC if v < 52 else KB
    if U_M3 <= u < U_M4:
        return DC if (u - U_M3) % 8 < 4 else 4
    return DC


def group(u):
    return u + (OFF_F1 if u < U_M1 else OFF_M if u < U_F2 else OFF_F2)


def load_of(u):
    if u < U_M3:
        return u // 2, u % 2
    return L_M3 + (u - U_M3) // 2, (u - U_M3) % 2


def load_unit(n):
    return 2 * n if n < L_M3 else U_M3 + 2 * (n - L_M3)


def load_incs(n):
    if n in (L_M1 + 6, L_M1 + 7):
        return 32
    if L_M3 <= n < L_M4 and (n - L_M3) % 4 == 3:
        return 32
    return 16


def raw_count(n):
    return sum(load_incs(k) for k in range(n % 2, n + 1, 2))


def build(nc, a):
    with ExitStack() as ctx:
        base = 16512

        def at(name, off, shape, dt=F32):
            return nc.alloc_sbuf_tensor_at(name, shape, dt, offset=base + off)

        def sem(name):
            return ctx.enter_context(nc.semaphore(name))

        CHB = T * 4
        X0, W0, T0 = 0, 3 * DC * CHB, 3 * DC * CHB + 2 * 12288 + 2 * 24576
        C0 = T0 + 8 * CHB
        xT = at("xT", X0, [P, DC, T])
        xh = at("xh", X0 + DC * CHB, [P, DC, T], F32R)
        xl = at("xl", X0 + 2 * DC * CHB, [P, DC, T], F32R)
        xg = at("xg", X0 + DC * CHB, [P, DC, T])
        raw = [at(f"raw{s}", W0 + 12288 * s, [P, KA, 2 * P]) for s in range(2)]
        whi = at("whi", W0 + 24576, [P, WS, KA, P], F32R)
        wlo = at("wlo", W0 + 49152, [P, WS, KA, P], F32R)
        tmp = [at(f"tmp{k}", T0 + CHB * k, [P, T]) for k in range(8)]
        ssq = tmp[7]
        sq = [tmp[6], tmp[4]]
        o = [C0]

        def small(name, shape, dt=F32):
            n = int(np.prod(shape[1:])) * 4
            t = at(name, o[0], shape, dt)
            o[0] += (n + 31) // 32 * 32
            return t

        ident = small("ident", [P, P])
        ones = small("ones", [P, P])
        cs = small("cs", [P, 2, T])
        srows = at("srows", C0 + 1024, [DB, 3 * ROW])
        tri = small("tri", [P, SEQ])
        kcS = small("kcS", [P, DB, NCMP])
        vcS = small("vcS", [NCMP, DB, P])
        rr = small("rr", [P, T])
        gn4 = small("gn4", [P, 4, DC])
        cw = small("cw", [P, 3, 4])
        sc = small("sc", [P, 4, 2, DB])
        tail = small("tail", [P, 4, 10])
        w2 = small("w2", [P, 2, HD])
        hpe = small("hpe", [P, 2])
        idx = small("idx", [P, DB], U32)
        ptab = small("ptab", [P, DB], I32)
        sub = small("sub", [P, 1])
        gt = small("gt", [P, QT, 24])
        gts = small("gts", [DB, 24])
        g64 = small("g64", [64, 3])
        valid = small("valid", [P, QT])
        cmask = small("cmask", [P, QT, PCMP])
        mcs = small("mcs", [NCMP, NSEL])
        e16 = small("e16", [16, 64])
        e8 = small("e8", [DB, 64])
        dmask = small("dmask", [64, DB * KVH])
        gmask = small("gmask", [64, KVH])
        kcP = small("kcP", [P, PCMP])
        vcP = small("vcP", [PCMP, P])
        st5 = small("st5", [P, 5])
        nmx = small("nmx", [P, 2, QT])
        lsm = small("lsm", [P, 2, QT])
        fct = small("fct", [P, 2, QT])
        cmx = small("cmx", [P, 2, QT])
        cfc = small("cfc", [P, 2, QT])
        sst = small("sst", [64, 16])
        bump = small("bump", [P, 2])
        zz = small("zz", [P, 64], F32R)
        rk16 = small("rk16", [16, NSEL])
        sb64 = small("sb64", [64, NSEL])
        A0 = (o[0] + 31) // 32 * 32
        HB = KA * CHB
        hh = at("hh", A0, [P, KA, T], F32R)
        hl = at("hl", A0 + HB, [P, KA, T], F32R)
        assert base + A0 + 2 * HB <= 229344, base + A0 + 2 * HB
        ub = at("ub", A0, [P, 4, T])
        ui = at("ui", A0 + 4 * CHB, [P, 4, T])
        vch = at("vch", A0, [P, 4, T], F32R)
        vcl = at("vcl", A0 + 4 * CHB, [P, 4, T], F32R)
        Q = at("Q", A0 + 8 * CHB, [P, 4, T])
        otl = at("otl", A0 + 8 * CHB, [P, 4, T], F32R)
        kv = at("kv", A0 + 12 * CHB, [P, 6, T])
        oth = at("oth", A0 + 12 * CHB, [P, 4, T], F32R)
        rows = at("rows", A0 + 18 * CHB, [P, QT, 3 * ROW])
        mm = at("mm", A0 + 16 * CHB, [P, DC, T])
        mh = at("mh", A0, [P, DC, T], F32R)
        ml = at("ml", A0 + 8 * CHB, [P, DC, T], F32R)
        XC = [at(f"XC{k}", X0 + 16384 * k, [NCH, CH, ROW]) for k in range(2)]
        XTH = [[at(f"XT{k}h{b}", (X0 + 32768, W0 + 24576)[k] + 8192 * b, [P, 8, NCH, KVH], F32R) for b in range(2)]
               for k in range(2)]
        XTL = [[at(f"XT{k}l{b}", (A0 + 8192 * b, W0 + 49152 - 8192 * b)[k], [P, 8, NCH, KVH], F32R) for b in range(2)]
               for k in range(2)]
        w1 = at("w1", W0, [P, 2, 16, P])
        w1h = at("w1h", W0 + 57344, [P, 2, 16, P], F32R)
        w1l = at("w1l", A0 + 16384, [P, 2, 16, P], F32R)
        xr = at("xr", A0 + 32768, [P, QT, D])
        xrs = at("xrs", T0, [DB, D])
        wpe = at("wpe", A0 + 32768, [P, 16, P])
        wps = at("wps", A0 + 40960, [P, 2, P])
        SH = [at(f"SH{k}", T0 + 4096 + 2048 * k, [P, KVH, NCMP]) for k in range(2)]
        per = at("per", T0 + 8192, [16, 2, P])
        pet = at("pet", T0 + 9216, [P, 2, 16])
        scr = at("scr", T0 + 10240, [DB, 2 * DCV])
        GB = [at(f"GB{k}", W0 + 16384 * k, [NCH, CH, ROW]) for k in range(2)]
        xcp = at("xcp", W0 + 43648, [PCH, CH, ROW])
        w1p = [at("w1pk", W0 + 60032, [P, 16, P]), at("w1pv", T0, [P, 16, P])]
        NPS = PAST + 1 + SEQ + P
        ps = at("ps", W0 + 32768, [64, NPS])
        pst = at("pst", W0 + 43648, [P, 21, 64])
        sm = [at(f"sm{k}", W0 + 49152 + 5120 * k, [P, QT * (QT + 1) // 2 * P]) for k in range(2)]
        ptp = at("ptp", W0 + 59392, [P, QT, SEQ])
        kt = [at(f"kt{k}", W0 + 68224 + 2048 * k, [P, SEQ]) for k in range(2)]
        xtp = [at(f"xtp{k}", W0 + 68224 + 2048 * k, [P, 8, KVH, PCH]) for k in range(2)]
        qp = at("qp", A0 + 12 * CHB, [P, DB, 72])
        wt = [at(f"wt{k}", T0 + 4096 * k, [P, 4, ROW]) for k in range(2)]
        qz = at("qz", T0 + 4 * CHB, [P, KVH, SEQ])
        ptc = at("ptc", T0 + 6 * CHB, [PCMP, SEQ])
        cm = [at(f"cm{k}", T0 + 7 * CHB + 512 * k, [P, QT, PCMP]) for k in range(2)]
        scs = at("scs", T0 + 7 * CHB + 1024, [64, 132])
        qps = [at(f"qps{k}", T0 + 7 * CHB + 1568 + 256 * k, [P, 64]) for k in range(2)]
        pcS = at("pcS", W0 + 49152, [NCMP, 16])
        scr16 = at("scr16", W0 + 49216, [16, NSEL])
        cmp3 = at("cmp3", W0 + 59392, [16, NSEL, NSEL])
        eq3 = at("eq3", W0 + 49984, [16, NSEL, NSEL])
        tie3 = at("tie3", W0 + 54368, [16, NSEL, NSEL])
        shp = [at(f"shp{k}", T0 + 7 * CHB + 512 * k, [P, KVH * PCMP]) for k in range(2)]
        trow = at("trow", T0 + 4 * CHB, [10, DCV])
        gnT = at("gnT", T0 + 7 * CHB, [24, T])
        zr = at("zr", T0 + 6 * CHB, [P, SEQ], F32R)
        o64 = at("o64", T0 + 7 * CHB + 1024, [64, P])
        om = at("om", T0 + 7 * CHB + 1568, [64, P])
        oT64 = at("oT64", T0, [P, 64])
        oS = at("oS", T0 + 256, [P, 32])
        yr = [at(f"yr{k}", A0 + 4096 * k, [P, D]) for k in range(QT + 1)]

        bank = ctx.enter_context(nc.psum_tensor("bank", [P, 8, 512], F32))

        def acc(g):
            return bank[:, 2 * (g % WS):2 * (g % WS) + 2, 0:HT]

        def flat(g, n, p=P):
            return bank[0:p, 2 * (g % WS):2 * (g % WS) + 2, :].rearrange("p a b -> p (a b)")[:, 0:n]

        def two(t):
            return t.rearrange("p (a b) -> p a b", a=2)

        def halves(xt, n):
            m = n % 4
            half, s = slice(HD * (m % 2), HD * (m % 2) + HD), m // 2 * 4
            for g in range(KVH):
                yield xt[half, s:s + 4, :, g], bank[HD * g:HD * (g + 1), m, :].rearrange("p (s c) -> p s c", s=4)

        gscr = nc.dram_tensor("gate_scratch", [DB, 24], F32, kind="Internal").ap()

        ident_loaded, const_loaded, ptab_loaded, cmpw_loaded, x_loaded = map(
            sem, ("ident_loaded", "const_loaded", "ptab_loaded", "cmpw_loaded", "x_loaded"))
        raw_loaded = [sem("raw0_loaded"), sem("raw1_loaded")]
        idx_ready = sem("idx_ready")
        xc_loaded = [sem("xc0_loaded"), sem("xc1_loaded")]
        gb_loaded = [sem("gb0_loaded"), sem("gb1_loaded")]
        xt_tp, xt_hi, xt_lo, w1_hi, w1_lo = map(sem, ("rows_turned", "rows_hi", "rows_lo", "w1_hi", "w1_lo"))
        w2_loaded, sq_ready, x_sum = map(sem, ("w2_loaded", "sq_ready", "x_sum"))
        w1_loaded = [sem("w1k_loaded"), sem("w1v_loaded")]
        hid_done, hid_act, cmp_done, cmp_ev = map(sem, ("hid_done", "hid_act", "cmp_done", "cmp_emptied"))
        pe_tp, pe_ev, pe_step, wps_ready, hpe_done, hpe_ready = map(
            sem, ("pe_turned", "pe_emptied", "pe_step", "wps_ready", "hpe_done", "hpe_ready"))
        hi_done, lo_done, grp_done, acc_free = map(sem, ("hi_done", "lo_done", "grp_done", "acc_free"))
        xh_done, xl_done, x_step, ssq_ready, std_ready, r_ready = map(
            sem, ("xh_done", "xl_done", "x_step", "ssq_ready", "std_ready", "r_ready"))
        silu_done, h_ready, hh_done, hl_done = map(sem, ("silu_done", "h_ready", "hh_done", "hl_done"))
        m_step, kv_ready, v_ready, vch_done, vcl_done, gn_sig = map(
            sem, ("m_step", "kv_ready", "v_ready", "vch_done", "vcl_done", "gn_sig"))
        sc_ready = sem("sc_ready")
        tp_done, tp_ev = sem("tp_done"), sem("tp_emptied")
        out_s, win_s, gscr_s, g64_loaded, xcp_loaded, tie_loaded = map(
            sem, ("out_stored", "win_stored", "gate_scratch_stored", "g64_loaded", "xcp_loaded", "tie_loaded"))
        w1p_loaded = [sem("w1pk_loaded"), sem("w1pv_loaded")]
        cph_done, cph_act, cpo_done, cpo_ev = map(sem, ("cph_done", "cph_act", "cpo_done", "cpo_emptied"))
        qp_ready, scm_done, scs_ready, sc_nm, sc_exp, pcn_ready, pct_done, pcs_ready, imp_done, selb_ready, selx_done = map(
            sem, ("qp_ready", "score_cmp_done", "scs_ready", "sc_nm", "sc_exp", "pcn_ready", "pct_done", "pcs_ready",
                  "imp_done", "selb_ready", "selx_done"))
        s_step, qps_ready, kt_used, zz_ready = map(sem, ("s_step", "qps_ready", "kt_used", "zz_ready"))
        wt_loaded = [sem("wt0_loaded"), sem("wt1_loaded")]
        snm, sexp, ps_ready = map(sem, ("sample_nm", "sample_exp", "ps_ready"))
        (qz_ready, big_s, cmp_s, big_rd, cmp_rd, big_nm, big_exp, big_p, cmp_nm, cmp_exp, cmp_p, pv_done, o_hi, o_lo,
         p_step) = map(
            sem, ("qz_ready", "big_scores", "cmp_scores", "big_read", "cmp_read", "big_nm", "big_exp", "big_p",
                  "cmp_nm", "cmp_exp", "cmp_p", "pv_done", "o_hi", "o_lo", "p_step"))
        keys_rd, sv_done, sv_rd, vn_done, o64_ready, o64_tp, os_hi = map(
            sem, ("keys_read", "sample_pv", "sample_pv_read", "vnew_done", "o64_ready", "o64_turned", "os_hi"))
        os_lo, ones_ready, gt_ready, mh_done, ml_done = map(sem, ("os_lo", "ones_ready", "gt_ready", "mh_done", "ml_done"))
        sig_done, m_ready = map(sem, ("sig_done", "m_ready"))
        fst_done, fms_ready, fstd_ready, fr_ready, xg_ready, y_tp, y_ev, y_out = map(
            sem, ("final_stats", "final_ms", "final_std", "final_r", "xg_ready", "y_turned", "y_emptied", "y_stored"))

        class Steps:

            def __init__(self, eng, s):
                self.eng, self.s, self.n, self.i, self.per = eng, s, 0, None, 0

            def did(self, ins):
                ins.then_inc(self.s, 1)
                self.n += 1
                return self.n

            def wait(self, n=None):
                n = self.n if n is None else n
                self.eng.wait_ge(self.s, n if self.i is None else n + self.i * self.per)

            def loop(self, i, per):
                self.i, self.per, self.first = i, per, self.n

            def end(self, times):
                assert self.n - self.first == self.per, (self.n - self.first, self.per)
                self.n = self.first + self.per * times
                self.i = None

        TB = 7
        TBC = TB + 40
        TBS = TBC + 2
        TBP = TBS + 3

        def load_pages(eng, first):
            for r in range(first, 8, 2):
                eng.dma_start(ptab[r:P - 7 + r:8, :], a["page_table"].rearrange("b p -> p b"),
                              allow_slow_non_contiguous=True).then_inc(ptab_loaded, 16)

        block = ctx.enter_context(nc.Block())

        @block.sync
        def _(sp):
            load_pages(sp, 0)
            sp.dma_start(sub[:, :], a["c_sub"]).then_inc(ptab_loaded, 16)
            sp.dma_start(ident[:, :], a["c_ident"]).then_inc(ident_loaded, 16)
            sp.dma_start(scr[:, :], a["state_conv"][0].rearrange("b k d -> b (k d)")).then_inc(cmpw_loaded, 16)
            for k, n in enumerate(("k", "v")):
                sp.dma_start(per[:, k, :], a[f"pe_cmp{n}"][0].rearrange("(j r) d -> j (r d)", r=2)).then_inc(cmpw_loaded, 16)
            for k, n in enumerate(("k", "v")):
                sp.dma_start(w1[:, k, :, :], a[f"w_cmp{n}1"][0].rearrange("r s d h -> (r s d) h")
                             .rearrange("(j p) h -> p j h", p=P)).then_inc(w1_loaded[k], 16)
            for k, n in enumerate(("k", "v")):
                sp.dma_start(w2[:, k, :], a[f"w_cmp{n}2"][0]).then_inc(w2_loaded, 16)
            for k, n in enumerate(("norm_ffn1", "norm_mix", "norm_ffn2", "norm_final")):
                src = a[n] if n == "norm_final" else a[n][0]
                sp.dma_start(gn4[:, k, :], src.rearrange("(c p) -> p c", p=P),
                             allow_slow_non_contiguous=True).then_inc(const_loaded, 16)
            for k in range(3):
                sp.dma_start(cw[:, k, :], a["conv_w"][0, k].rearrange("(c p) -> p c", p=P),
                             allow_slow_non_contiguous=True).then_inc(const_loaded, 16)
            for t, n in ((cmask, "c_cmask"), (tri, "c_tri"), (valid, "c_valid"), (mcs, "c_mcs"), (e16, "c_e16"),
                         (e8, "c_e8"), (dmask, "c_dmask"), (gmask, "c_gmask"), (cs, "c_cs")):
                sp.dma_start(t[:], a[n]).then_inc(const_loaded, 16)
            sp.wait_ge(hpe_done, 1)
            sp.dma_start(xr[:, :, :], a["x_prompt"][0].rearrange("(t p) d -> p t d", p=P)).then_inc(x_loaded, 16)
            sp.dma_start(xrs[:, :], a["x_sample"][:, 0, :]).then_inc(x_loaded, 16)

            def slot_free(n, i=None, units=0):
                if n < 2 and i is None:
                    return
                u = load_unit(n - 1) if i is None else load_unit(n) - 2
                sp.wait_ge(lo_done, u if i is None else u + i * units)

            def ffn_loads(n0, gate, up, down):
                for first, k, iters in ((0, KA, KA // 2), (KA, KB, KB // 2)):
                    for m in range(2):
                        slot_free(n0 + m)
                        sp.dma_start(raw[(n0 + m) % 2][:, 0:DC, :], (gate, up)[m][:, :, first * P:(first + 2) * P])\
                            .then_inc(raw_loaded[(n0 + m) % 2], 16)
                    with sp.Fori(1, iters) as i:
                        for m in range(2):
                            src = (gate, up)[m][:, :, first * P:][:, :, bass.ds(i * (2 * P), 2 * P)]
                            slot_free(n0 + m, i, 4)
                            sp.dma_start(raw[(n0 + m) % 2][:, 0:DC, :], src).then_inc(raw_loaded[(n0 + m) % 2], 16)
                    n0 += 2 * iters
                    rows_ = down[first * P:(first + k) * P, :].rearrange("(k p) n -> p k n", p=P)
                    for m in range(4):
                        slot_free(n0 + m)
                        sp.dma_start(raw[(n0 + m) % 2][:, 0:k, :], rows_[:, :, 2 * P * m:2 * P * (m + 1)])\
                            .then_inc(raw_loaded[(n0 + m) % 2], 16)
                    n0 += 4

            def kview(w):
                return w.rearrange("(k p) n -> p k n", p=P)

            sp.wait_ge(w1_lo, 2)
            ffn_loads(L_F1, kview(a["ffn1_w_gate"][0]), kview(a["ffn1_w_up"][0]), a["ffn1_w_down"][0])
            sp.dma_start(a["win_kv_sample"][0, :, 0:SEQ - 1], a["state_win_kv"][0, :, 1:SEQ]).then_inc(win_s, 16)
            sp.dma_start(a["conv_sample"][0, :, 0, :], a["state_conv"][0, :, 1, :]).then_inc(out_s, 16)
            wm = kview(a["w_mix_in"][0])
            for m in range(12):
                n = L_M1 + m
                slot_free(n)
                s = n % 2
                if m in (6, 7):
                    for g in range(KVH):
                        c = C_Q + g * HPG * HD + (m - 6) * P
                        sp.dma_start(raw[s][:, 0:DC, g * P:(g + 1) * P], wm[:, :, c:c + P]).then_inc(raw_loaded[s], 16)
                elif m < 11:
                    sp.dma_start(raw[s][:, 0:DC, :], wm[:, :, 2 * P * m:2 * P * (m + 1)]).then_inc(raw_loaded[s], 16)
                else:
                    sp.dma_start(raw[s][:, 0:DC, 0:24], wm[:, :, C_GN:C_GB]).then_inc(raw_loaded[s], 16)
            sp.wait_ge(tp_ev, 4)
            for r, nm in enumerate(("cmp_kv_prompt", "sel_kv_prompt", "win_kv_prompt")):
                sp.dma_start(a[nm].rearrange("l b (t p) c h d -> p (l b t) (c h d)", p=P),
                             rows[:, :, r * ROW:(r + 1) * ROW]).then_inc(xcp_loaded if r == 0 else out_s, 16)
            sp.wait_ge(grp_done, group(U_M3 - 1) + 1)
            sp.dma_start(tie3[:], a["c_tie"]).then_inc(tie_loaded, 16)
            sp.wait_ge(tp_ev, 5)
            for r, nm in enumerate(("cmp_kv_sample", "sel_kv_sample")):
                sp.dma_start(a[nm].rearrange("l b t c h d -> (l b t) (c h d)"), srows[:, r * ROW:(r + 1) * ROW])\
                    .then_inc(out_s, 16)
            sp.dma_start(a["win_kv_sample"][0, :, SEQ - 1].rearrange("b c h d -> b (c h d)"), srows[:, 2 * ROW:3 * ROW])\
                .then_inc(win_s, 16)
            sp.wait_ge(tp_ev, 6)
            sp.dma_start(a["conv_prompt"][0, 0], trow[0:2, :]).then_inc(out_s, 16)
            sp.dma_start(a["conv_sample"][0, :, 1, :], trow[2:10, :]).then_inc(out_s, 16)
            sp.wait_ge(tp_ev, 7)
            sp.dma_start(gscr, gts[:, :]).then_inc(gscr_s, 16)
            sp.wait_ge(gscr_s, 16)
            sp.dma_start(g64[:, :], gscr.rearrange("b (h c) -> (b h) c", c=3)).then_inc(g64_loaded, 16)
            sp.wait_ge(win_s, 32)
            wv = a["win_kv_sample"][0].rearrange("b (t p) c h d -> p b t (c h d)", p=P)
            for s in range(2):
                sp.dma_start(wt[s][:, :, :], wv[:, s, :, :]).then_inc(wt_loaded[s], 16)
            with sp.Fori(0, 3) as i:
                for s in range(2):
                    sp.wait_ge(tp_done, i * 10 + (TB + 5 * s + 5))
                    sp.dma_start(wt[s][:, :, :], wv[:, bass.ds(i * 2 + (2 + s), 1), :, :]
                                 .rearrange("p b t e -> p (b t) e")).then_inc(wt_loaded[s], 16)
            w1v = [a[f"w_cmp{n}1"][0].rearrange("r s d h -> (r s d) h").rearrange("(j p) h -> p j h", p=P) for n in ("k", "v")]
            sp.wait_ge(selb_ready, 1)
            sp.wait_ge(xcp_loaded, 16)
            sp.dma_start(xcp[:], a["cmp_kv_prompt"].rearrange("l b (t s) c h d -> (l b t) s (c h d)", s=CH))\
                .then_inc(xcp_loaded, 16)
            sp.dma_start(w1p[0][:, :, :], w1v[0]).then_inc(w1p_loaded[0], 16)
            sp.wait_ge(tp_done, TBC)
            sp.dma_start(w1p[1][:, :, :], w1v[1]).then_inc(w1p_loaded[1], 16)
            sp.wait_ge(cph_done, 2)
            for s in range(2):
                sp.dma_start(wt[s][:, :, :], wv[:, s, :, :]).then_inc(wt_loaded[s], 16)
            with sp.Fori(0, 3) as i:
                for s in range(2):
                    sp.wait_ge(sv_done, i * 2 + (s + 1))
                    sp.dma_start(wt[s][:, :, :], wv[:, bass.ds(i * 2 + (2 + s), 1), :, :]
                                 .rearrange("p b t e -> p (b t) e")).then_inc(wt_loaded[s], 16)
            sp.wait_ge(sv_done, DB - 1)
            wc = kview(a["w_conv_out"][0])
            wa = a["w_attn_out"][0].rearrange("(g j p) n -> g p j n", g=KVH, p=HD)

            def m3(i, n):
                def cols(w):
                    return w[:, :, 0:2 * P] if i is None else w[:, :, 2 * P:][:, :, bass.ds(i * (2 * P), 2 * P)]

                for m, w in enumerate((wm[:, :, C_GB:], wm[:, :, C_GB + D:], wc)):
                    src = cols(w)
                    if i is None and m == 1:
                        sp.wait_ge(sv_done, DB)
                    slot_free(n + m, i, 8)
                    sp.dma_start(raw[(n + m) % 2][:, 0:DC if m < 2 else 4, :], src).then_inc(raw_loaded[(n + m) % 2], 16)
                s = (n + 3) % 2
                src = [cols(wa[g]) for g in range(KVH)]
                slot_free(n + 3, i, 8)
                for g in range(KVH):
                    sp.dma_start(raw[s][HD * g:HD * (g + 1), 0:4, :], src[g]).then_inc(raw_loaded[s], 16)

            m3(None, L_M3)
            with sp.Fori(0, 3) as i:
                m3(i, L_M3 + 4)
            wo = kview(a["w_mix_out"][0])
            for m in range(4):
                slot_free(L_M4 + m)
                sp.dma_start(raw[(L_M4 + m) % 2][:, 0:DC, :], wo[:, :, 2 * P * m:2 * P * (m + 1)])\
                    .then_inc(raw_loaded[(L_M4 + m) % 2], 16)
            ffn_loads(L_F2, kview(a["ffn2_w_gate"][0]), kview(a["ffn2_w_up"][0]), a["ffn2_w_down"][0])
            for t in range(QT + 1):
                sp.wait_ge(y_ev, t + 1)
                if t < QT:
                    sp.dma_start(a["y_prompt"][0, t * P:(t + 1) * P, :], yr[t][:, :]).then_inc(y_out, 16)
                else:
                    sp.dma_start(a["y_sample"][:, 0, :], yr[t][0:DB, :]).then_inc(y_out, 16)
            sp.wait_ge(y_out, 16 * (QT + 1))
            sp.wait_ge(out_s, 16 * 7)
            sp.wait_ge(win_s, 32)

        @block.gpsimd
        def _(pool):
            pool.memset(ones[:, :], 1.0).then_inc(ones_ready, 1)
            caches = [a[n][0].rearrange("n (u s) c h d -> (n u) (s c h d)", s=CH) for n in ("cache_cmp_kv", "cache_sel_kv")]

            def gather(dst, which, b, s):
                pool.indirect_dma_start(dst[:].rearrange("p s e -> p (s e)"), None, caches[which],
                                        bass.IndirectOffsetOnAxis(idx[:, b:b + 1], 0)).then_inc(s, 16)

            def lo(u, i=None, per=0):
                n, half = load_of(u)
                k, c = phase_of(u), cols(u)
                pool.wait_ge(hi_done, u + 1 if i is None else i * per + (u + 1))
                w = u % WS
                pool.tensor_tensor(tile(wlo, w, k, u), raw_tile(u), tile(whi, w, k, u).bitcast(F32), ALU.subtract)\
                    .then_inc(lo_done, 1)

            def cols(u):
                return 24 if u == U_M3 - 1 else P

            def tile(t, w, k, u):
                v = t[:, w, 0:k, 0:cols(u)]
                return v.rearrange("p k (g d) -> p k g d", g=KVH) if U_M1 + 12 <= u < U_M1 + 16 else v

            def raw_tile(u):
                n, half = load_of(u)
                r = raw[n % 2][:, 0:phase_of(u), :]
                if U_M1 + 12 <= u < U_M1 + 16:
                    return r.rearrange("p k (g u d) -> p k g u d", g=KVH, u=2)[:, :, :, half, :]
                return r[:, :, half * P:half * P + cols(u)]

            pool.wait_ge(idx_ready, 1)
            for b in range(2):
                gather(XC[b], 0, b, xc_loaded[b])
            for k in range(2):
                pool.wait_ge(w1_hi, k + 1)
                pool.tensor_tensor(w1l[:, k, :, :], w1[:, k, :, :], w1h[:, k, :, :].bitcast(F32), ALU.subtract).then_inc(w1_lo, 1)
            for b in range(2, DB):
                pool.wait_ge(xt_tp, 8 * (b - 1))
                gather(XC[b % 2], 0, b, xc_loaded[b % 2])
            for c in range(DC):
                pool.wait_ge(acc_free, G_X + c + 1)
                if c >= 3:
                    pool.wait_ge(x_sum, c - 2)
                pool.tensor_tensor((ssq if c == 0 else sq[c % 2])[:, :], xT[:, c, :], xT[:, c, :], ALU.mult).then_inc(sq_ready, 1)
                if c == 3:
                    lo(U_F1)

            def ffn_lo(u0):
                for iters in (KA // 2, KB // 2):
                    peeled = u0 == U_F1
                    if peeled:
                        for j in range(1, 4):
                            lo(u0 + j)
                    with pool.Fori(1 if peeled else 0, iters) as i:
                        for j in range(4):
                            lo(u0 + j, i, 4)
                    u0 += 4 * iters
                    with pool.Fori(0, 2) as i:
                        for j in range(4):
                            lo(u0 + j, i, 4)
                    u0 += 8

            ffn_lo(U_F1)
            for u in range(U_M1, U_M3):
                lo(u)
            for v in range(2):
                for b in range(DB):
                    if v == 0 and b == 0:
                        pool.wait_ge(lo_done, U_M3)
                    elif v == 0 and b == 1:
                        pool.wait_ge(grp_done, group(U_M3 - 2) + 1)
                    elif v == 0:
                        pool.wait_ge(tp_done, TB + 5 * (b - 1))
                    elif b < 2:
                        pool.wait_ge(tp_done, TB + 5 * (DB - 1 + b))
                    else:
                        pool.wait_ge(sv_done, b - 1)
                    gather(GB[b % 2], 1, b, gb_loaded[b % 2])
            with pool.Fori(0, 4) as i:
                for j in range(8):
                    if j == 1:
                        pool.wait_ge(tp_done, TBP + 18 * (HPG - 1) + 14)
                    if j == 2:
                        pool.wait_ge(pv_done, 6 * HPG)
                    lo(U_M3 + j, i, 8)
            for u in range(U_M4, U_F2):
                lo(u)
            ffn_lo(U_F2)

        @block.scalar
        def _(act):
            def cols(u):
                return 24 if u == U_M3 - 1 else P

            def hi(u, i=None, per=0):
                n, half = load_of(u)
                k = phase_of(u)
                if half == 0:
                    r = raw_count(n)
                    if i is None:
                        act.wait_ge(raw_loaded[n % 2], r)
                    else:
                        step = raw_count(n + per // 2) - r
                        act.wait_ge(raw_loaded[n % 2], i * step + r)
                if u >= WS:
                    g = group(u - WS) + 1
                    act.wait_ge(grp_done, g if i is None else i * per + g)
                dst = whi[:, u % WS, 0:k, 0:cols(u)]
                src = raw[n % 2][:, 0:k, :]
                if U_M1 + 12 <= u < U_M1 + 16:
                    dst = dst.rearrange("p k (g d) -> p k g d", g=KVH)
                    src = src.rearrange("p k (g u d) -> p k g u d", g=KVH, u=2)[:, :, :, half, :]
                else:
                    src = src[:, :, half * P:half * P + cols(u)]
                act.activation(dst, src, ACT.Copy).then_inc(hi_done, 1)

            load_pages(act, 1)
            act.wait_ge(pe_tp, 1)
            act.activation(pet[:, :, :].rearrange("p k j -> p (k j)"), bank[:, 4, 0:32], ACT.Copy).then_inc(pe_ev, 1)
            act.activation(sc[:, :, :, :].rearrange("p c k b -> p k c b"),
                           bank[:, 4, 64:128].rearrange("p (k c b) -> p k c b", k=2, c=4), ACT.Copy).then_inc(sc_ready, 1)

            def split_w1(k):
                act.wait_ge(w1_loaded[k], 16)
                act.activation(w1h[:, k, :, :], w1[:, k, :, :], ACT.Copy).then_inc(w1_hi, 1)

            split_w1(0)

            def split_x(k, c):
                act.activation(xh[:, c, :], xT[:, c, :], ACT.Copy, scale=gn4[:, k, c:c + 1]).then_inc(xh_done, 1)

            def first_x(c0, c1):
                for c in range(c0, c1):
                    act.wait_ge(grp_done, G_X + c + 1)
                    act.activation(xT[:, c, :], flat(c % 2, T), ACT.Copy).then_inc(acc_free, 1)
                    act.wait_ge(acc_free, G_X + c + 1)
                    split_x(0, c)

            def rows_hi(n, i=0):
                for n in range(n, n + 4):
                    act.wait_ge(xt_tp, i * 16 + (n + 1))
                    for dst, src in halves(XTH[n // 4 % 2][n // 8 % 2], n):
                        ins = act.activation(dst, src, ACT.Copy)
                    ins.then_inc(xt_hi, 1)

            def hidden(kk, b, i=0):
                act.wait_ge(hid_done, i * 4 + (2 * b + kk + 1))
                act.activation(SH[kk][:, :, :], bank[:, 4 + kk, 0:KVH * NCMP].rearrange("p (c g) -> p g c", g=KVH), ACT.Silu,
                               bias=hpe[:, kk:kk + 1]).then_inc(hid_act, 1)

            rows_hi(0)
            rows_hi(4)
            split_w1(1)
            rows_hi(8)
            act.wait_ge(hpe_done, 1)
            act.activation(hpe[:, :], bank[:, 6, 0:2], ACT.Copy).then_inc(hpe_ready, 1)
            act.wait_ge(hpe_ready, 1)
            hidden(0, 0)
            with act.Fori(0, DB // 2 - 1) as i:
                for b in range(2):
                    rows_hi(8 * b + 12, i)
                    hidden(1, b, i)
                    rows_hi(8 * b + 16, i)
                    hidden(0, b + 1, i)
            rows_hi(8 * DB - 4)
            hidden(1, DB - 2)
            act.wait_ge(const_loaded, 16 * 16)
            first_x(0, 3)
            hi(0)
            first_x(3, 4)
            hidden(0, DB - 1)
            first_x(4, DC)
            hidden(1, DB - 1)
            act.wait_ge(cmp_done, 2 * DB)
            for u in range(1, 4):
                hi(u)

            def root(k):
                act.wait_ge(acc_free, G_ST[k] + 1)
                act.activation(tmp[5][:, :], tmp[5][:, :], ACT.Sqrt).then_inc(std_ready, 1)

            def ffn(u0, nk, h0):
                for half, iters in enumerate((KA // 2, KB // 2)):
                    def body(i, last):
                        for j in range(4):
                            u = u0 + j
                            if last:
                                hi(u + 4 * iters)
                            else:
                                hi(u + 4, i, 4)
                            e = (iters - 1) * 4 if last else i * 4
                            e2 = (iters - 1) * 2 if last else i * 2
                            if j < 2:
                                act.wait_ge(acc_free, e + (group(u) + 1))
                                act.activation(tmp[j][:, :], tmp[j][:, :], ACT.Silu).then_inc(silu_done, 1)
                            else:
                                act.wait_ge(h_ready, e2 + (h0 + j - 1))
                                c = (iters - 1) * 2 + j - 2 if last else i * 2 + (j - 2)
                                dst = hh[:, c, :] if last else hh[:, bass.ds(c, 1), :].rearrange("p o t -> p (o t)")
                                act.activation(dst, tmp[1 + j][:, :], ACT.Copy).then_inc(hh_done, 1)
                    with act.Fori(0, iters - 1) as i:
                        body(i, False)
                    body(None, True)
                    u0 += 4 * iters
                    h0 += 2 * iters
                    for d in range(DC):
                        if u0 + d + 4 < U_END:
                            hi(u0 + d + 4)
                        if half == 1 and nk is not None:
                            act.wait_ge(acc_free, group(u0 + d) + 1)
                            split_x(nk, d)
                    u0 += DC

            root(0)
            ffn(U_F1, 1, 0)
            root(1)
            for t in range(23):
                if U_M1 + t + 4 < U_M3:
                    hi(U_M1 + t + 4)
                if 8 <= t < 12:
                    c = t - 8
                    act.wait_ge(v_ready, c + 1)
                    act.activation(vch[:, c, :], tmp[2 + c % 2][:, :], ACT.Copy).then_inc(vch_done, 1)
            act.wait_ge(acc_free, group(U_M3 - 1) + 1)
            act.activation(gnT[:, :], gnT[:, :], ACT.Sigmoid).then_inc(gn_sig, 1)
            for t in range(QT):
                act.wait_ge(tp_done, t + 1)
                act.activation(rows[:, t, :], bank[:, 2 * t:2 * t + 2, :].rearrange("p a b -> p (a b)")[:, 0:3 * ROW], ACT.Copy)\
                    .then_inc(tp_ev, 1)
            act.wait_ge(tp_done, 5)
            act.activation(srows[:, :], bank[0:DB, 0:2, :].rearrange("p a b -> p (a b)")[:, 0:3 * ROW], ACT.Copy).then_inc(tp_ev, 1)
            act.wait_ge(tp_done, 6)
            act.activation(trow[:, :], bank[0:10, 2, :], ACT.Copy).then_inc(tp_ev, 1)
            act.wait_ge(tp_done, 7)
            act.activation(gt[:, :, :].rearrange("p t e -> p (t e)"), bank[:, 3, 0:96], ACT.Copy).then_inc(gt_ready, 1)
            act.activation(gts[:, :], bank[0:DB, 3, 96:120], ACT.Copy).then_inc(tp_ev, 1)
            act.wait_ge(sc_nm, 1)
            act.activation(ps[:, PAST + 1 + SEQ:PAST + 1 + SEQ + NCMP], scs[:, 0:NCMP], ACT.Exp, bias=sst[:, 1:2], scale=SCALE,
                           accum_out=sst[:, 2:3]).then_inc(sc_exp, 1)
            with act.Fori(0, DB // 2) as i:
                for q in range(10):
                    act.wait_ge(tp_done, i * 10 + (TB + q + 1))
                    act.wait_ge(kt_used, i * 10 + (q + 1))
                    act.activation(kt[q % 2][:, :], bank[:, 6 + q % 2, :], ACT.Copy).then_inc(tp_ev, 1)
            for kk in range(2):
                act.wait_ge(tp_done, TBC + kk + 1)
                for r in range(2):
                    for g in range(KVH):
                        src = bank[HD * g:HD * (g + 1), 6 + kk, :].rearrange("p (s r c) -> p s r c", r=2, c=PCH)[:, :, r, :]
                        ins = act.activation(xtp[kk][HD * r:HD * (r + 1), :, g, :], src, ACT.Copy)
                ins.then_inc(tp_ev, 1)
            act.wait_ge(snm, 1)
            act.activation(ps[:, 0:PAST + 1], ps[:, 0:PAST + 1], ACT.Exp, bias=sst[:, 5:6], scale=SCALE,
                           accum_out=sst[:, 6:7]).then_inc(sexp, 1)
            act.wait_ge(snm, 2)
            act.activation(ps[:, PAST + 1:PAST + 1 + SEQ], bank[0:64, 4, :], ACT.Exp, bias=sst[:, 9:10], scale=SCALE,
                           accum_out=sst[:, 10:11]).then_inc(sexp, 1)

            for kk in range(2):
                act.wait_ge(cph_done, kk + 1)
                act.activation(shp[kk][:, :], bank[:, 5 + kk, 0:KVH * PCMP], ACT.Silu, bias=hpe[:, kk:kk + 1]).then_inc(cph_act, 1)
            act.wait_ge(cpo_done, 1)
            act.activation(kcP[:, :], bank[:, 7, 0:PCMP], ACT.Copy).then_inc(cpo_ev, 1)
            act.wait_ge(cpo_done, 2)
            act.activation(vcP[:, :], bank[0:PCMP, 5, P:2 * P], ACT.Copy).then_inc(cpo_ev, 1)
            def empty(b, j, nxt=0):
                t = [0, 1, 5, 9, 10, 14][b] + 18 * nxt
                if b:
                    act.wait_ge(pv_done, j * 6 + b)
                if b % 3 == 0:
                    act.wait_ge(tp_done, j * 18 + (TBP + t + 1))
                    act.activation(ptc[:, :], bank[0:PCMP, 4 + t % 2, :], ACT.Copy).then_inc(tp_ev, 1)
                    return
                for q in range(QT):
                    act.wait_ge(tp_done, j * 18 + (TBP + t + q + 1))
                    act.activation(ptp[:, 0:q + 1, q * P:(q + 1) * P],
                                   bank[:, 4 + (t + q) % 2, 0:(q + 1) * P].rearrange("p (k n) -> p k n", n=P), ACT.Copy)\
                        .then_inc(tp_ev, 1)

            def exps(b, j, nxt=0):
                if b % 3 == 0:
                    act.wait_ge(cmp_nm, j * 2 + (2 * nxt + b // 3 + 1))
                    act.activation(cm[b // 3][:], cm[b // 3][:], ACT.Exp, scale=SCALE).then_inc(cmp_exp, 1)
                    return
                n = b - 1 - b // 3
                act.wait_ge(big_nm, j * 4 + (4 * nxt + n + 1))
                for q in range(QT):
                    v = sm[n % 2][:, q * (q + 1) // 2 * P:(q + 1) * (q + 2) // 2 * P]
                    act.activation(v, v, ACT.Exp, bias=nmx[:, n % 2, q:q + 1], scale=SCALE,
                                   accum_out=lsm[:, n % 2, q:q + 1]).then_inc(big_exp, 1)

            def attend(j, last):
                for b in range(1, 5):
                    exps(b + 1, j)
                    if last and b == 4:
                        act.wait_ge(sv_done, DB)
                        hi(U_M3)
                    empty(b, j)
                if last:
                    hi(U_M3 + 1)
                empty(5, j)
                if not last:
                    exps(0, j, 1)
                    exps(1, j, 1)
                act.wait_ge(pv_done, j * 6 + 6)
                act.activation(oth[:, bass.ds(j, 1), 0:SEQ].rearrange("p o t -> p (o t)"), bank[:, 6, :], ACT.Copy)\
                    .then_inc(o_hi, 1)
                if not last:
                    empty(0, j, 1)

            exps(0, 0)
            for n, m in enumerate((8, 8, 5)):
                act.wait_ge(tp_done, TBS + n + 1)
                act.activation(pst[:, 8 * n:8 * n + m, :].rearrange("p s e -> p (s e)"), bank[:, (5, 4, 6)[n], 0:64 * m], ACT.Copy).then_inc(tp_ev, 1)
            exps(1, 0)
            empty(0, 0)
            with act.Fori(0, HPG - 1) as j:
                attend(j, False)
            attend(HPG - 1, True)
            for u in range(2, 4):
                hi(U_M3 + u)
                if u == 2:
                    act.wait_ge(o64_ready, 2)
                    act.activation(oth[:, :, SEQ:T].rearrange("p j b -> p b j"), oS[:, :].rearrange("p (b j) -> p b j", j=4),
                                   ACT.Copy).then_inc(os_hi, 1)

            def m3(i):
                for k in range(8):
                    u = U_M3 + k
                    if i is not None:
                        hi(u + 4, i, 8)
                    else:
                        hi(u + 4 + 24 if k < 4 else U_M4 + k - 4)
                    if k < 4:
                        act.wait_ge(acc_free, (24 if i is None else i * 8) + (group(u) + 1))
                        act.activation(tmp[k][:, :], tmp[k][:, :], ACT.Sigmoid).then_inc(sig_done, 1)

            with act.Fori(0, 3) as i:
                m3(i)
            m3(None)
            act.wait_ge(grp_done, group(U_M4 - 1) + 1)
            for d in range(DC):
                act.wait_ge(m_ready, d + 1)
                act.activation(mh[:, d, :], mm[:, d, :], ACT.Copy).then_inc(mh_done, 1)
            for d in range(DC):
                hi(U_M4 + 4 + d)
                act.wait_ge(acc_free, group(U_M4 + d) + 1)
                split_x(2, d)
            root(2)
            ffn(U_F2, None, DFC)
            act.wait_ge(fms_ready, 1)
            act.activation(st5[:, :], st5[:, :], ACT.Sqrt).then_inc(fstd_ready, 1)
            act.wait_ge(fr_ready, 1)
            for t in range(QT + 1):
                p = P if t < QT else DB
                act.wait_ge(y_tp, t + 1)
                act.activation(yr[t][0:p, :], flat(t + 2, D, p), ACT.Copy,
                               scale=st5[0:p, t:t + 1]).then_inc(y_ev, 1)

        @block.vector
        def _(dve):
            tt, ts, stt = dve.tensor_tensor, dve.tensor_scalar, dve.scalar_tensor_tensor
            dve.wait_ge(ptab_loaded, 16 * 9)
            ts(idx[:, :], ptab[:, :], float(PAGE // CH), sub[:, 0:1], ALU.mult, ALU.add).then_inc(idx_ready, 1)
            def rows_lo(n, i=0):
                for n in range(n, n + 4):
                    dve.wait_ge(xt_hi, i * 16 + (n + 1))
                    pair = n // 4 % 2, n // 8 % 2
                    for (dst, src), (hi_, _) in zip(halves(XTL[pair[0]][pair[1]], n), halves(XTH[pair[0]][pair[1]], n)):
                        ins = tt(dst, src, hi_.bitcast(F32), ALU.subtract)
                    ins.then_inc(xt_lo, 1)

            def compressed(kk, b, i=0):
                dve.wait_ge(cmp_done, i * 4 + (2 * b + kk + 1))
                dst, src = ((kcS, bank[:, 6, 0:NCMP]), (vcS, bank[0:NCMP, 7, 0:P]))[kk]
                dve.tensor_copy(dst[:, bass.ds(i * 2 + b, 1), :].rearrange("p o c -> p (o c)"), src).then_inc(cmp_ev, 1)

            es = Steps(dve, pe_step)
            dve.wait_ge(pe_ev, 1)
            for k in range(2):
                if k:
                    rows_lo(0)
                    rows_lo(4)
                dve.wait_ge(w1_loaded[k], 16)
                es.did(tt(wpe[:, :, :], w1[:, k, :, :], pet[:, k, :].unsqueeze(2).to_broadcast([P, 16, P]), ALU.mult))
                es.wait()
                dve.tensor_reduce(wps[:, k, :], wpe[:, :, :].rearrange("p j h -> p h j"), AX.X, ALU.add).then_inc(wps_ready, 1)
                dve.wait_ge(wps_ready, k + 1)
            rows_lo(8)
            with dve.Fori(0, DB // 2 - 1) as i:
                for b in range(2):
                    rows_lo(8 * b + 12, i)
                    compressed(0, b, i)
                    rows_lo(8 * b + 16, i)
                    compressed(1, b, i)
            rows_lo(8 * DB - 4)
            xs = Steps(dve, x_step)
            XL = (0, DC, 2 * DC)

            def prep(k, c):
                dst = ssq if c == 0 else tmp[6]
                ins = tt(dst[:, :], xT[:, c, :], xT[:, c, :], ALU.mult)
                if c:
                    xs.did(ins)
                    xs.wait()
                    ins = tt(ssq[:, :], ssq[:, :], tmp[6][:, :], ALU.add)
                if c == DC - 1:
                    ins.then_inc(ssq_ready, 1)
                else:
                    xs.did(ins)
                if k < 3:
                    dve.wait_ge(xh_done, XL[k] + c + 1)
                    stt(xl[:, c, :], xT[:, c, :], gn4[:, k, c:c + 1], xh[:, c, :].bitcast(F32), ALU.mult, ALU.subtract)\
                        .then_inc(xl_done, 1)
                else:
                    ts(xg[:, c, :], xT[:, c, :], gn4[:, k, c:c + 1], None, ALU.mult).then_inc(xg_ready, 1)
                if c < DC - 1:
                    xs.wait()

            def stats(k):
                g = G_ST[k]
                dve.wait_ge(grp_done, g + 2)
                ts(two(tmp[5][:, :]), acc(g), 1.0 / D, EPS, ALU.mult, ALU.add).then_inc(acc_free, 1)
                dve.wait_ge(std_ready, k + 1)
                dve.reciprocal(rr[:, :], tmp[5][:, :]).then_inc(r_ready, 1)
                dve.wait_ge(r_ready, k + 1)

            def first_x(c0, c1):
                for c in range(c0, c1):
                    if c:
                        dve.wait_ge(sq_ready, c + 1)
                        if c > 1:
                            dve.wait_ge(x_sum, c - 1)
                        tt(ssq[:, :], ssq[:, :], sq[c % 2][:, :], ALU.add).then_inc(x_sum if c < DC - 1 else ssq_ready, 1)
                    dve.wait_ge(xh_done, c + 1)
                    stt(xl[:, c, :], xT[:, c, :], gn4[:, 0, c:c + 1], xh[:, c, :].bitcast(F32), ALU.mult, ALU.subtract)\
                        .then_inc(xl_done, 1)

            compressed(0, DB - 2)
            compressed(1, DB - 2)
            first_x(0, 3)
            compressed(0, DB - 1)
            first_x(3, DC)
            compressed(1, DB - 1)
            stats(0)

            def ffn(u0, nk, h0):
                for half, iters in enumerate((KA // 2, KB // 2)):
                    with dve.Fori(0, iters) as i:
                        for j in range(4):
                            g = group(u0 + j)
                            dve.wait_ge(grp_done, i * 4 + (g + 1))
                            dst = tmp[j] if j < 2 else tmp[2]
                            tt(two(dst[:, :]), acc(g), two(rr[:, :]), ALU.mult).then_inc(acc_free, 1)
                            if j >= 2:
                                dve.wait_ge(acc_free, i * 4 + (g + 1))
                                dve.wait_ge(silu_done, i * 2 + (h0 + j - 1))
                                tt(tmp[1 + j][:, :], tmp[j - 2][:, :], tmp[2][:, :], ALU.mult).then_inc(h_ready, 1)
                                dve.wait_ge(hh_done, i * 2 + (h0 + j - 1))
                                c = bass.ds(i * 2 + (j - 2), 1)
                                tt(hl[:, c, :].rearrange("p o t -> p (o t)"), tmp[1 + j][:, :],
                                   hh[:, c, :].rearrange("p o t -> p (o t)").bitcast(F32), ALU.subtract).then_inc(hl_done, 1)
                    u0 += 4 * iters
                    h0 += 2 * iters
                    for d in range(DC):
                        g = group(u0 + d)
                        dve.wait_ge(grp_done, g + 1)
                        stt(two(xT[:, d, :]), acc(g), 0.5, two(xT[:, d, :]), ALU.mult, ALU.add).then_inc(acc_free, 1)
                        if half == 1:
                            dve.wait_ge(acc_free, g + 1)
                            prep(nk, d)
                    u0 += DC

            ffn(U_F1, 1, 0)
            stats(1)

            ms = Steps(dve, m_step)
            for k in range(2):
                ms.did(tt(cs[:, k, :], cs[:, k, :], rr[:, :], ALU.mult))
            ms.wait()

            def scaled(dst, t, p=P):
                g = group(U_M1 + t)
                dve.wait_ge(grp_done, g + 1)
                tt(two(dst), acc(g)[0:p], two(rr[0:p, :]), ALU.mult).then_inc(acc_free, 1)
                return g + 1

            def rope(dst, t):
                g = group(U_M1 + t)
                dve.wait_ge(grp_done, g + 1)
                ms.wait()
                ms.did(tt(two(tmp[4][:, :]), acc(g), two(cs[:, 0, :]), ALU.mult))
                for q in range(4):
                    s, d = slice(32 * q, 32 * q + 32), slice(32 * (q ^ 1), 32 * (q ^ 1) + 32)
                    ins = tt(two(tmp[5][d, :]), acc(g)[s], two(cs[s, 1, :]), ALU.mult)
                    if q < 3:
                        ms.did(ins)
                ins.then_inc(acc_free, 1)
                dve.wait_ge(acc_free, g + 1)
                ms.wait()
                ms.did(tt(dst, tmp[4][:, :], tmp[5][:, :], ALU.add))

            dve.wait_ge(sc_ready, 1)
            for t in range(4):
                scaled(ub[:, t, :], t)
            for t in range(4, 8):
                scaled(ui[:, t - 4, :], t)
            for c in range(4):
                dve.wait_ge(acc_free, scaled(tmp[0][:, :], 8 + c))
                u, y, v = ui[:, c, :], tmp[1], tmp[2 + c % 2]

                def tap(k):
                    return cw[:, k, c:c + 1]

                ms.did(tt(u, tmp[0][:, :], u, ALU.mult))
                ms.wait()
                ms.did(dve.tensor_copy(tail[:, c, :], u[:, SEQ - 2:T]))
                ms.did(ts(y[:, :], u, tap(2), None, ALU.mult))
                ms.wait()
                ms.did(stt(y[:, 2:SEQ], u[:, 0:SEQ - 2], tap(0), y[:, 2:SEQ], ALU.mult, ALU.add))
                ms.did(stt(y[:, SEQ:T], sc[:, c, 0, :], tap(0), y[:, SEQ:T], ALU.mult, ALU.add))
                ms.wait()
                ms.did(stt(y[:, 1:SEQ], u[:, 0:SEQ - 1], tap(1), y[:, 1:SEQ], ALU.mult, ALU.add))
                ms.did(stt(y[:, SEQ:T], sc[:, c, 1, :], tap(1), y[:, SEQ:T], ALU.mult, ALU.add))
                ms.wait()
                tt(v[:, :], y[:, :], ub[:, c, :], ALU.mult).then_inc(v_ready, 1)
                dve.wait_ge(vch_done, c + 1)
                tt(vcl[:, c, :], v[:, :], vch[:, c, :].bitcast(F32), ALU.subtract).then_inc(vcl_done, 1)
            for j in range(4):
                rope(Q[:, j, :], 12 + j)
            for t in range(3):
                rope(kv[:, 3 + t, :], 16 + 2 * t)
                scaled(kv[:, t, :], 17 + 2 * t)
            scaled(gnT[:, :], 22, 24)
            dve.wait_ge(acc_free, group(U_M3 - 1) + 1)
            ms.wait()
            dve.memset(bump[:, 1:2], 0.0).then_inc(kv_ready, 1)

            st = Steps(dve, s_step)
            dve.wait_ge(tp_done, 7)
            st.did(dve.memset(qp[:, :, :], 0.0))
            ts(zz[:, :], tri[:, 0:64], 0.0, None, ALU.mult).then_inc(zz_ready, 1)
            ts(zr[:, :], tri[:, :], 0.0, None, ALU.mult).then_inc(zz_ready, 1)
            st.wait()
            for g in range(KVH):
                ins = dve.tensor_copy(qp[HD * g:HD * (g + 1), :, HPG * g:HPG * (g + 1)],
                                      Q[HD * g:HD * (g + 1), :, SEQ:T].rearrange("p j b -> p b j"))
            ins.then_inc(qp_ready, 1)
            dve.wait_ge(qp_ready, 1)
            for b in range(2):
                dve.tensor_copy(qps[b][:, :], qp[:, :, :].rearrange("p b c -> p (b c)")[:, 64 * b:64 * b + 64]).then_inc(qps_ready, 1)
            dve.wait_ge(scm_done, 1)
            dve.tensor_copy(scs[:, 0:P + 1], bank[0:64, 5, 0:P + 1]).then_inc(scs_ready, 1)
            dve.wait_ge(scs_ready, 1)

            def neg_max(src, c, s, v):
                st.did(dve.tensor_reduce(sst[:, c:c + 1], src, AX.X, ALU.max, negate=True))
                st.wait()
                ts(sst[:, c + 1:c + 2], sst[:, c:c + 1], SCALE, None, ALU.mult).then_inc(s, 1)

            neg_max(scs[:, 0:NCMP], 0, sc_nm, 1)
            dve.wait_ge(sc_exp, 1)
            st.did(dve.reciprocal(sst[:, 3:4], sst[:, 2:3]))
            st.wait()
            pcmp = ps[:, PAST + 1 + SEQ:PAST + 1 + SEQ + NCMP]
            ts(pcmp, pcmp, sst[:, 3:4], None, ALU.mult).then_inc(pcn_ready, 1)
            dve.wait_ge(pct_done, 1)
            dve.tensor_reduce(pcS[:, :], bank[0:NCMP, 5, 0:64].rearrange("p (a h) -> p a h", h=HPG), AX.X, ALU.add)\
                .then_inc(pcs_ready, 1)
            dve.wait_ge(imp_done, 1)
            st.did(dve.tensor_copy(scr16[:, :], bank[0:16, 5, 0:NSEL]))
            st.wait()
            st.did(dve.memset(scr16[:, 0:1], BIG))
            st.did(dve.memset(scr16[:, NSEL - 2:NSEL], BIG))
            st.wait()
            s_i = scr16[:, :].unsqueeze(1).to_broadcast([16, NSEL, NSEL])
            s_j = scr16[:, :].unsqueeze(2).to_broadcast([16, NSEL, NSEL])
            dve.wait_ge(tie_loaded, 16)
            st.did(tt(cmp3[:], s_i, s_j, ALU.is_gt))
            st.did(tt(eq3[:], s_i, s_j, ALU.is_equal))
            st.wait()
            st.did(tt(eq3[:], eq3[:], tie3[:], ALU.mult))
            st.wait()
            st.did(tt(cmp3[:], cmp3[:], eq3[:], ALU.add))
            st.wait()
            st.did(dve.tensor_reduce(rk16[:, :], cmp3[:], AX.X, ALU.add))
            st.wait()
            st.did(ts(rk16[:, :], rk16[:, :], float(TOP), 1.0, ALU.is_lt, ALU.subtract))
            st.wait()
            ts(rk16[:, :], rk16[:, :], -NEG, None, ALU.mult).then_inc(selb_ready, 1)
            dve.wait_ge(out_s, 16 * 7)
            dve.memset(qz[:, :, :], 0.0).then_inc(o_lo, 1)
            dve.wait_ge(o_lo, 1)

            def queries(j, nxt=0):
                for g in range(KVH):
                    ins = dve.tensor_copy(qz[HD * g:HD * (g + 1), g, :],
                                          Q[HD * g:HD * (g + 1), bass.ds(j + nxt, 1), 0:SEQ].rearrange("p o t -> p (o t)"))
                ins.then_inc(qz_ready, 1)

            queries(0)
            for b in range(2, DB):
                dve.wait_ge(kt_used, 2 + 5 * (b - 1))
                dve.tensor_copy(qps[b % 2][:, :], qp[:, :, :].rearrange("p b c -> p (b c)")[:, 64 * b:64 * b + 64]).then_inc(qps_ready, 1)
            dve.wait_ge(gt_ready, 1)
            g0 = gt[:, :, :].rearrange("p t (h c) -> p t h c", c=3)[:, :, :, 0]
            st.did(tt(g0, g0, valid[:, :].unsqueeze(2).to_broadcast([P, QT, NH]), ALU.mult))
            dve.wait_ge(selx_done, 1)
            st.did(dve.tensor_copy(sb64[:, :], bank[0:64, 5, 0:NSEL]))
            st.wait()
            tt(ps[:, 0:PAST].rearrange("p (s k c) -> p s k c", s=CH, c=4),
               bank[0:64, 0:4, :].rearrange("p a b -> p (a b)").rearrange("p (s k c) -> p s k c", s=CH, c=4),
               sb64[:, 0:NSEL - 1].unsqueeze(1).unsqueeze(3).to_broadcast([64, CH, NSEL - 1, 4]), ALU.add).then_inc(keys_rd, 1)
            dve.wait_ge(keys_rd, 1)
            st.did(dve.tensor_copy(ps[:, PAST:PAST + 1], scs[:, P:P + 1]))
            st.wait()
            neg_max(ps[:, 0:PAST + 1], 4, snm, 1)
            neg_max(bank[0:64, 4, :], 8, snm, 2)
            dve.wait_ge(g64_loaded, 16)
            dve.wait_ge(sexp, 2)
            for k, (lo_, n) in enumerate(((0, PAST + 1), (PAST + 1, SEQ))):
                l, f = sst[:, 6 + 4 * k:7 + 4 * k], sst[:, 12 + k:13 + k]
                st.did(dve.reciprocal(f, l))
                st.wait()
                st.did(tt(f, f, g64[:, 1 + k:2 + k], ALU.mult))
                st.wait()
                v = ps[:, lo_:lo_ + n]
                st.did(ts(v, v, f, None, ALU.mult))
            ts(pcmp, pcmp, g64[:, 0:1], None, ALU.mult).then_inc(ps_ready, 1)
            st.wait()
            st.did(dve.tensor_copy(sst[:, 15:16], ps[:, PAST:PAST + 1]))
            st.did(dve.memset(o64[:, :], 0.0))

            pp = Steps(dve, p_step)

            def stage1(b, j, nxt=0):
                if b % 3 == 0:
                    g = b // 3
                    dve.wait_ge(cmp_s, j * 2 + (2 * nxt + g + 1))
                    dve.wait_ge(tp_done, j * 18 + (18 * nxt + TBP - 18 + 1 + 9 * g))
                    c = cm[g]
                    tt(c[:], bank[:, 7, 0:QT * PCMP].rearrange("p (q n) -> p q n", n=PCMP), cmask[:], ALU.add).then_inc(cmp_rd, 1)
                    dve.wait_ge(cmp_rd, j * 2 + (2 * nxt + g + 1))
                    pp.did(dve.tensor_reduce(cmx[:, g, :], c[:], AX.X, ALU.max))
                    pp.wait()
                    tt(c[:], c[:], cmx[:, g, :].unsqueeze(2).to_broadcast([P, QT, PCMP]), ALU.subtract).then_inc(cmp_nm, 1)
                    return
                n = b - 1 - b // 3
                dve.wait_ge(tp_done, j * 18 + (18 * nxt + TBP + (14 - 18, 18 - 18, 5, 9)[n]))
                dve.wait_ge(big_s, j * 16 + (16 * nxt + 4 * n + 4))
                dve.memset(bump[:, 0:1], 0.0)
                for q in range(QT):
                    dve.tensor_tensor_reduce(sm[n % 2][:, q * (q + 1) // 2 * P:(q + 1) * (q + 2) // 2 * P],
                                             bank[:, q, 0:(q + 1) * P], tri[:, SEQ - (q + 1) * P:SEQ], 1.0, -3e38,
                                             ALU.add, ALU.max, nmx[:, n % 2, q:q + 1])\
                        .then_inc(big_rd, 1)
                dve.wait_ge(big_rd, j * 16 + (16 * nxt + 4 * n + 4))
                ts(nmx[:, n % 2, :], nmx[:, n % 2, :], -SCALE, None, ALU.mult).then_inc(big_nm, 1)

            def stage2(b, j, nxt=0):
                g = b // 3
                gate = gt[:, :, bass.ds(j * 3 + (3 * nxt + 12 * g + b % 3), 1)].rearrange("p t o -> p (t o)")
                if b % 3 == 0:
                    c = cm[g]
                    dve.wait_ge(cmp_exp, j * 2 + (2 * nxt + g + 1))
                    pp.did(dve.tensor_reduce(cfc[:, g, :], c[:], AX.X, ALU.add))
                    pp.wait()
                    pp.did(dve.reciprocal(cfc[:, g, :], cfc[:, g, :]))
                    pp.wait()
                    pp.did(tt(cfc[:, g, :], cfc[:, g, :], gate, ALU.mult))
                    pp.wait()
                    tt(c[:], c[:], cfc[:, g, :].unsqueeze(2).to_broadcast([P, QT, PCMP]), ALU.mult).then_inc(cmp_p, 1)
                    return
                n = b - 1 - g
                dve.wait_ge(big_exp, j * 16 + (16 * nxt + 4 * n + 4))
                pp.did(dve.reciprocal(fct[:, n % 2, :], lsm[:, n % 2, :]))
                pp.wait()
                pp.did(tt(fct[:, n % 2, :], fct[:, n % 2, :], gate, ALU.mult))
                pp.wait()
                for q in range(QT):
                    v = sm[n % 2][:, q * (q + 1) // 2 * P:(q + 1) * (q + 2) // 2 * P]
                    ts(v, v, fct[:, n % 2, q:q + 1], None, ALU.mult).then_inc(big_p, 1)

            def sampled(j, s):
                dve.wait_ge(sv_done, j * 2 + (s + 1))
                tt(om[:, :].rearrange("p (g d) -> p g d", g=KVH), bank[0:64, 7, 2 * P:3 * P].rearrange("p (g d) -> p g d", g=KVH),
                   dmask[:, bass.ds(j * 4 + 2 * s, 2)].unsqueeze(2).to_broadcast([64, KVH, HD]), ALU.mult).then_inc(sv_rd, 1)
                dve.wait_ge(sv_rd, j * 2 + (s + 2))
                pp.did(tt(o64[:, :], o64[:, :], om[:, :], ALU.add))

            def attend(j, last):
                if not last:
                    pp.loop(j, 18)
                for b in range(1, 6):
                    if b in (3, 5):
                        stage2(b, j)
                    if b < 5:
                        stage1(b + 1, j)
                    elif not last:
                        stage1(0, j, 1)
                    if b not in (3, 5):
                        stage2(b, j)
                    if b in (1, 4):
                        sampled(j, b // 3)
                    if b == 4 and not last:
                        dve.wait_ge(big_s, j * 16 + 16)
                        queries(j, 1)
                if not last:
                    stage2(0, j, 1)
                    stage1(1, j, 1)
                else:
                    dve.wait_ge(vn_done, 1)
                    pp.wait()
                    pp.did(ts(om[:, :], bank[0:64, 7, 3 * P:4 * P], sst[:, 15:16], None, ALU.mult))
                    pp.wait()
                    omg = om[:, :].rearrange("p (g d) -> p g d", g=KVH)
                    pp.did(tt(omg, omg, gmask[:, :].unsqueeze(2).to_broadcast([64, KVH, HD]), ALU.mult))
                    pp.wait()
                    tt(o64[:, :], o64[:, :], om[:, :], ALU.add).then_inc(o64_ready, 1)
                dve.wait_ge(o_hi, j + 1)
                tt(otl[:, bass.ds(j, 1), 0:SEQ].rearrange("p o t -> p (o t)"), bank[:, 6, :],
                   oth[:, bass.ds(j, 1), 0:SEQ].rearrange("p o t -> p (o t)").bitcast(F32), ALU.subtract).then_inc(o_lo, 1)
                if not last:
                    pp.end(HPG - 1)

            dve.memset(bump[:, 0:1], 0.0).then_inc(sv_rd, 1)
            stage1(0, 0)
            stage2(0, 0)
            stage1(1, 0)
            with dve.Fori(0, HPG - 1) as j:
                attend(j, False)
            attend(HPG - 1, True)

            dve.wait_ge(o64_tp, 1)
            st.did(dve.tensor_copy(oT64[:, :], bank[:, 7, 0:64]))
            st.wait()
            pair = oT64[:, :].rearrange("p (b g j) -> p b g j", b=DB, g=KVH)
            tt(oS[:, :].rearrange("p (b j) -> p b j", j=HPG), pair[:, :, 0, :], pair[:, :, 1, :], ALU.add).then_inc(o64_ready, 1)
            dve.wait_ge(os_hi, 1)
            tt(otl[:, :, SEQ:T].rearrange("p j b -> p b j"), oS[:, :].rearrange("p (b j) -> p b j", j=HPG),
               oth[:, :, SEQ:T].rearrange("p j b -> p b j").bitcast(F32), ALU.subtract).then_inc(os_lo, 1)
            dve.wait_ge(os_lo, 1)

            with dve.Fori(0, 4) as i:
                for k in range(8):
                    g = group(U_M3 + k)
                    dve.wait_ge(grp_done, i * 8 + (g + 1))
                    if k < 4:
                        tt(two(tmp[k][:, :]), acc(g), two(rr[:, :]), ALU.mult).then_inc(acc_free, 1)
                        continue
                    dve.wait_ge(sig_done, i * 4 + (k - 3))
                    if k < 6:
                        tt(two(tmp[k - 4][:, :]), acc(g), two(tmp[k - 4][:, :]), ALU.mult).then_inc(acc_free, 1)
                    else:
                        tt(two(tmp[k - 2][:, :]), acc(g), two(tmp[k - 4][:, :]), ALU.mult).then_inc(acc_free, 1)
                        dve.wait_ge(acc_free, i * 8 + (g + 1))
                        tt(mm[:, bass.ds(i * 2 + (k - 6), 1), :].rearrange("p o t -> p (o t)"), tmp[k - 6][:, :], tmp[k - 2][:, :],
                           ALU.add).then_inc(m_ready, 1)
                dve.wait_ge(m_ready, i * 2 + 2)
            for d in range(DC):
                dve.wait_ge(mh_done, d + 1)
                tt(ml[:, d, :], mm[:, d, :], mh[:, d, :].bitcast(F32), ALU.subtract).then_inc(ml_done, 1)
            for d in range(DC):
                g = group(U_M4 + d)
                dve.wait_ge(grp_done, g + 1)
                tt(two(xT[:, d, :]), acc(g), two(xT[:, d, :]), ALU.add).then_inc(acc_free, 1)
                dve.wait_ge(acc_free, g + 1)
                prep(2, d)
            stats(2)
            ffn(U_F2, 3, DFC)
            dve.wait_ge(fst_done, 1)
            ts(st5[:, :], bank[:, 2, 0:5], 1.0 / D, EPS, ALU.mult, ALU.add).then_inc(fms_ready, 1)
            dve.wait_ge(fstd_ready, 1)
            dve.reciprocal(st5[:, :], st5[:, :]).then_inc(fr_ready, 1)

        @block.tensor
        def _(pe):
            def turn(dst, src):
                n = src.shape[0]
                return pe.transpose(dst, src, ident[0:n, 0:n])

            pe.wait_ge(cmpw_loaded, 16 * 3)
            pe.wait_ge(ident_loaded, 16)
            for k in range(2):
                turn(bank[:, 4, 16 * k:16 * k + 16], per[:, k, :])
            for k in range(8):
                ins = turn(bank[:, 4, 64 + 8 * k:72 + 8 * k], scr[:, k * P:(k + 1) * P])
            ins.then_inc(pe_tp, 1)

            def turn_rows(n, i=0):
                b, kk, m = n // 8 % 2, n // 4 % 2, n % 4
                if m == 0 and kk == 0:
                    pe.wait_ge(xc_loaded[b], i * 16 + (n // 16 * 16 + 16))
                if n >= 4:
                    pe.wait_ge(xt_lo, i * 16 + (n - 3))
                for t in range(4):
                    ins = turn(bank[:, m, t * P:(t + 1) * P], XC[b][:, 8 * (m // 2) + m % 2 + 2 * t, kk * P:(kk + 1) * P])
                ins.then_inc(xt_tp, 1)

            def second(kk, b, i=0, last=False):
                pe.wait_ge(hid_act, i * 4 + (2 * b + kk + 1))
                if last:
                    pe.wait_ge(cmp_ev, 2 * b + kk - 1)
                for g in range(KVH):
                    if kk == 0:
                        ins = pe.matmul(bank[HD * g:HD * (g + 1), 6, 0:NCMP], w2[:, 0, :], SH[0][:, g, :], start=True, stop=True)
                    else:
                        ins = pe.matmul(bank[0:NCMP, 7, g * HD:(g + 1) * HD], SH[1][:, g, :], w2[:, 1, :], start=True, stop=True)
                ins.then_inc(cmp_done, 1)

            def turn_x(c):
                if c == 0:
                    pe.wait_ge(x_loaded, 32)
                    pe.wait_ge(xt_lo, 8 * DB)
                if c >= 2:
                    pe.wait_ge(acc_free, c - 1)
                v = flat(c % 2, T)
                for t in range(QT):
                    turn(v[:, t * P:(t + 1) * P], xr[:, t, c * P:(c + 1) * P])
                turn(v[:, SEQ:T], xrs[:, c * P:(c + 1) * P]).then_inc(grp_done, 1)

            def first(kk, b, i=0, rows=None, other=None, chunk=None):
                hid = bank[:, 4 + kk, 0:KVH * NCMP]
                for s in range(8):
                    if s % 4 == 0:
                        pe.wait_ge(xt_lo, i * 16 + (8 * b + 4 * kk + s // 2 + 2))
                    for r in range(2):
                        j = 8 * r + s
                        for n, (w, x) in enumerate(((w1h, XTH), (w1h, XTL), (w1l, XTH))):
                            ins = pe.matmul(hid, w[:, kk, j, :], x[kk][b % 2][:, s, r:r + NCMP, :].rearrange("p c g -> p (c g)"),
                                            start=(s + r + n == 0), stop=(s == 7 and r == 1 and n == 2))
                    if s == 3 and other is not None:
                        second(*other, i, last=rows is None)
                    if s == 7 and chunk is not None:
                        ins.then_inc(hid_done, 1)
                    if s % 2 and chunk is not None:
                        turn_x(chunk + s // 2)
                    if s % 2 and rows is not None and s < 7:
                        turn_rows(rows + s // 2, i)
                if chunk is None:
                    ins.then_inc(hid_done, 1)
                if rows is not None:
                    turn_rows(rows + 3, i)

            for n in range(8):
                turn_rows(n)
            pe.wait_ge(sc_ready, 1)
            pe.wait_ge(w1_lo, 1)
            pe.wait_ge(w2_loaded, 32)
            first(0, 0, rows=8)
            pe.wait_ge(wps_ready, 2)
            pe.wait_ge(ones_ready, 1)
            for k in range(2):
                ins = pe.matmul(bank[:, 6, k:k + 1], wps[:, k, :], ones[:, 0:1], start=True, stop=True)
            ins.then_inc(hpe_done, 1)
            pe.wait_ge(w1_lo, 2)
            with pe.Fori(0, DB // 2 - 1) as i:
                for b in range(2):
                    first(1, b, i, 8 * b + 12, (0, b))
                    first(0, b + 1, i, 8 * b + 16, (1, b))
            first(1, DB - 2, rows=8 * DB - 4, other=(0, DB - 2))
            first(0, DB - 1, other=(1, DB - 2), chunk=0)
            first(1, DB - 1, other=(0, DB - 1), chunk=4)
            def stats(k):
                g = G_ST[k]
                pe.wait_ge(ones_ready, 1)
                pe.wait_ge(ssq_ready, k + 1)
                pe.wait_ge(acc_free, g - WS + 1)
                for h in range(2):
                    ins = pe.matmul(acc(g)[:, h, :], ones[:, :], ssq[:, h * HT:(h + 1) * HT], start=True, stop=True)
                ins.then_inc(grp_done, 1)

            def unit(u, xhi, xlo, i=None, per=0, ready=None, before=0, between=None):
                g, k = group(u), phase_of(u)
                m = 24 if u == U_M3 - 1 else P
                pe.wait_ge(lo_done, u + 1 if i is None else i * per + (u + 1))
                pe.wait_ge(acc_free, g - WS + 1 if i is None else i * per + (g - WS + 1))
                for c in range(k):
                    if between is not None and c == k // 2:
                        between()
                    if ready:
                        pe.wait_ge(ready, before + c + 1)
                    for n, (w, x) in enumerate(((whi, xhi), (whi, xlo), (wlo, xhi))):
                        for h in range(2):
                            ins = pe.matmul(acc(g)[0:m, h, :], w[:, u % WS, c, 0:m], x[:, c, h * HT:(h + 1) * HT],
                                            start=(c == 0 and n == 0), stop=(c == k - 1 and n == 2))
                ins.then_inc(grp_done, 1)

            def after_norm(u0, k, between=None):
                for j in range(4):
                    if j == 0:
                        unit(u0, xh, xl, ready=xl_done, before=k * DC, between=between)
                        stats(k)
                    else:
                        unit(u0 + j, xh, xl)

            def ffn(u0, k, h0, between=None):
                after_norm(u0, k, between)
                for half, iters in enumerate((KA // 2, KB // 2)):
                    with pe.Fori(1 - half, iters) as i:
                        for j in range(4):
                            unit(u0 + j, xh, xl, i, 4)
                    u0 += 4 * iters
                    h0 += 2 * iters
                    with pe.Fori(0, 2) as i:
                        for j in range(4):
                            unit(u0 + j, hh, hl, i, 4, hl_done if j == 0 else None, h0 - 2 * iters)
                    u0 += DC

            def last_compressed():
                second(1, DB - 1, last=True)
                pe.wait_ge(cmp_ev, 2 * DB)

            pe.wait_ge(acc_free, DC)
            ffn(U_F1, 0, 0, last_compressed)
            after_norm(U_M1, 1)
            with pe.Fori(1, 5) as i:
                for j in range(4):
                    unit(U_M1 + j, xh, xl, i, 4)
            for t in range(20, 23):
                unit(U_M1 + t, xh, xl)

            pe.wait_ge(acc_free, group(U_M3 - 1) + 1)
            pe.wait_ge(kv_ready, 1)
            order = (3, 0, 4, 1, 5, 2)

            def rows_of(bk, cols, p):
                v = bank[0:p, bk:bk + 2, :].rearrange("p a b -> p (a b)")
                for e, c in enumerate(order):
                    ins = turn(v[:, e * P:(e + 1) * P], kv[:, c, cols])
                ins.then_inc(tp_done, 1)

            for t in range(QT):
                rows_of(2 * t, slice(t * P, (t + 1) * P), P)
            pe.wait_ge(tp_ev, 1)
            rows_of(0, slice(SEQ, T), DB)
            pe.wait_ge(tp_ev, 2)
            for c in range(4):
                ins = turn(bank[0:10, 2, c * P:(c + 1) * P], tail[:, c, :])
            ins.then_inc(tp_done, 1)
            pe.wait_ge(gn_sig, 1)
            for t in range(QT):
                turn(bank[:, 3, 24 * t:24 * t + 24], gnT[:, t * P:(t + 1) * P])
            turn(bank[0:DB, 3, 96:120], gnT[:, SEQ:T]).then_inc(tp_done, 1)
            pe.wait_ge(qp_ready, 1)
            pe.wait_ge(tp_ev, 3)
            qpf = qp[:, :, :].rearrange("p b c -> p (b c)")
            for b in range(DB):
                pe.matmul(bank[0:64, 5, 0:NCMP], qpf[:, 64 * b:64 * b + 64], kcS[:, b, :], start=(b == 0), stop=(b == DB - 1))
            for b in range(DB):
                ins = pe.matmul(bank[0:64, 5, P:P + 1], qpf[:, 64 * b:64 * b + 64], kv[:, 4, SEQ + b:SEQ + b + 1], start=(b == 0), stop=(b == DB - 1))
            ins.then_inc(scm_done, 1)
            pe.wait_ge(zz_ready, 2)
            pe.wait_ge(tp_ev, TB)
            for k in range(5):
                ins = pe.matmul(bank[0:64, k, :], zz[:, :], zr[:, :], start=True, stop=False)
            ins.then_inc(kt_used, 2)

            pe.wait_ge(pcn_ready, 1)
            turn(bank[0:NCMP, 5, 0:64], ps[:, PAST + 1 + SEQ:PAST + 1 + SEQ + NCMP]).then_inc(pct_done, 1)
            pe.wait_ge(pcs_ready, 1)
            pe.matmul(bank[0:16, 5, 0:NSEL], pcS[:, :], mcs[:, :], start=True, stop=True).then_inc(imp_done, 1)

            def turn_keys(q, i):
                s = q // 5
                if q % 5 == 0:
                    pe.wait_ge(gb_loaded[s], i * 16 + 16)
                if q % 5 == 4:
                    pe.wait_ge(wt_loaded[s], i * 16 + 16)
                pe.wait_ge(tp_ev, i * 10 + (TB + q - 1))
                for t in range(4):
                    src = wt[s][:, t, 0:P] if q % 5 == 4 else GB[s][:, 4 * (q % 5) + t, 0:P]
                    ins = turn(bank[:, 6 + q % 2, t * P:(t + 1) * P], src)
                ins.then_inc(tp_done, 1)

            def score_keys(q, i):
                if q % 5 == 0:
                    pe.wait_ge(qps_ready, i * 2 + (q // 5 + 1))
                pe.wait_ge(tp_ev, i * 10 + (TB + q + 1))
                pe.matmul(bank[0:64, q % 5, :], qps[q // 5][:, :], kt[q % 2][:, :], start=False, stop=False,
                          skip_group_check=True).then_inc(kt_used, 1)

            with pe.Fori(0, DB // 2) as i:
                turn_keys(0, i)
                for q in range(10):
                    if q < 9:
                        turn_keys(q + 1, i)
                    score_keys(q, i)
            for k in range(5):
                pe.matmul(bank[0:64, k, :], zz[:, :], zr[:, :], start=False, stop=True)
            pe.wait_ge(selb_ready, 1)
            pe.matmul(bank[0:64, 5, 0:NSEL], e16[:, :], rk16[:, :], start=True, stop=True).then_inc(selx_done, 1)

            pe.wait_ge(xcp_loaded, 32)
            for kk in range(2):
                pe.wait_ge(tp_ev, TBC - 1 + kk)
                for s in range(CH):
                    ins = turn(bank[:, 6 + kk, s * PCH:(s + 1) * PCH], xcp[:, s, kk * P:(kk + 1) * P])
                ins.then_inc(tp_done, 1)
            for kk in range(2):
                pe.wait_ge(tp_ev, TBC + kk + 1)
                pe.wait_ge(w1p_loaded[kk], 16)
                if kk == 0:
                    pe.wait_ge(keys_rd, 1)
                for r in range(2):
                    for s in range(8):
                        ins = pe.matmul(bank[:, 5 + kk, 0:KVH * PCMP].rearrange("p (g c) -> p g c", g=KVH), w1p[kk][:, 8 * r + s, :],
                                        xtp[kk][:, s, :, r:r + PCMP], start=(r + s == 0), stop=(r == 1 and s == 7))
                ins.then_inc(cph_done, 1)
            pe.wait_ge(cph_act, 1)
            for g in range(KVH):
                ins = pe.matmul(bank[HD * g:HD * (g + 1), 7, 0:PCMP], w2[:, 0, :], shp[0][:, g * PCMP:(g + 1) * PCMP], start=True, stop=True)
            ins.then_inc(cpo_done, 1)
            pe.wait_ge(cph_act, 2)
            for g in range(KVH):
                ins = pe.matmul(bank[0:PCMP, 5, P + g * HD:P + (g + 1) * HD], shp[1][:, g * PCMP:(g + 1) * PCMP], w2[:, 1, :], start=True, stop=True)
            ins.then_inc(cpo_done, 1)
            def scores(b, j, nxt=0):
                g = b // 3
                if b % 3 == 0:
                    if g or nxt:
                        pe.wait_ge(cmp_rd, j * 2 + (1 + nxt))
                        pe.wait_ge(sv_rd, j * 2 + (2 + nxt))
                    for q in range(QT):
                        ins = pe.matmul(bank[:, 7, q * PCMP:(q + 1) * PCMP], qz[:, g, q * P:(q + 1) * P], kcP[:, :], start=True, stop=True)
                    ins.then_inc(cmp_s, 1)
                    return
                n = b - 1 - g
                k = kv[:, 3 + b % 3, :]
                for q in range(QT):
                    if n or nxt:
                        pe.wait_ge(big_rd, j * 16 + (16 * nxt + 4 * n - 4 + q + 1))
                    pe.matmul(bank[:, q, 0:(q + 1) * P], qz[:, g, q * P:(q + 1) * P], k[:, 0:(q + 1) * P], start=True, stop=True)\
                        .then_inc(big_s, 1)

            def turns(b, j):
                t = [0, 1, 5, 9, 10, 14][b]
                if b % 3 == 0:
                    pe.wait_ge(cmp_p, j * 2 + (b // 3 + 1))
                    pe.wait_ge(tp_ev, j * 18 + (TBP + t - 1))
                    for q in range(QT):
                        ins = turn(bank[0:PCMP, 4 + t % 2, q * P:(q + 1) * P], cm[b // 3][:, q, :])
                    ins.then_inc(tp_done, 1)
                    return
                n = b - 1 - b // 3
                for q in range(QT):
                    pe.wait_ge(big_p, j * 16 + (4 * n + q + 1))
                    pe.wait_ge(tp_ev, j * 18 + (TBP + t + q - 1))
                    for k in range(q + 1):
                        c = q * (q + 1) // 2 * P + k * P
                        ins = turn(bank[:, 4 + (t + q) % 2, k * P:(k + 1) * P], sm[n % 2][:, c:c + P])
                    ins.then_inc(tp_done, 1)

            def values(b, j):
                g, t = b // 3, [1, 5, 9, 10, 14, 18][b]
                pe.wait_ge(tp_ev, j * 18 + (TBP + t))
                out = bank[HD * g:HD * (g + 1), 6, :]
                if b % 3 == 0:
                    if g == 0:
                        pe.wait_ge(o_lo, j + 1)
                    pe.matmul(out, vcP[:, g * HD:(g + 1) * HD], ptc[:, :], start=True, stop=False).then_inc(pv_done, 1)
                    return
                for k in reversed(range(QT)):
                    c = (b % 3) * ROW + P + g * HD
                    ins = pe.matmul(out[:, k * P:SEQ], rows[:, k, c:c + HD], ptp[:, k, k * P:SEQ], start=False,
                                    stop=(b % 3 == 2 and k == 0))
                ins.then_inc(pv_done, 1)

            def sampled(j, s):
                pe.wait_ge(gb_loaded[s], j * 16 + 16 * 5)
                pe.wait_ge(wt_loaded[s], j * 16 + 16 * 5)
                pe.wait_ge(cmp_rd, j * 2 + (1 + s))
                pe.wait_ge(sv_rd, j * 2 + (s + 1))
                out = bank[0:64, 7, 2 * P:3 * P]
                for t in range(16):
                    pe.matmul(out, pst[:, t, :], GB[s][:, t, P:2 * P], start=(t == 0), stop=False)
                for t in range(4):
                    pe.matmul(out, pst[:, 16 + t, :], wt[s][:, t, P:2 * P], start=False, stop=False)
                pe.matmul(out, pst[0:NCMP, 20, :], vcS[:, bass.ds(j * 2 + s, 1), :].rearrange("p o e -> p (o e)"),
                          start=False, stop=True).then_inc(sv_done, 1)

            def attend(j, last):
                for b in range(6):
                    if last and b == 5:
                        pe.wait_ge(big_rd, 16 * HPG)
                        unit(U_M3, xh, xl)
                    turns(b, j)
                    if b < 4:
                        scores(b + 2, j)
                    elif not last:
                        if b == 4:
                            pe.wait_ge(qz_ready, j + 2)
                        scores(b - 4, j, 1)
                    if b == 0:
                        sampled(j, 0)
                    values(b, j)
                    if b == 3:
                        sampled(j, 1)
                    if b == 4 and last:
                        pe.wait_ge(sv_rd, 1 + DB)
                        pe.matmul(bank[0:64, 7, 3 * P:4 * P], e8[:, :], srows[:, ROW + P:2 * ROW], start=True, stop=True)\
                            .then_inc(vn_done, 1)

            pe.wait_ge(qz_ready, 1)
            pe.wait_ge(cpo_ev, 2)
            scores(0, 0)
            pe.wait_ge(keys_rd, 1)
            scores(1, 0)
            pe.wait_ge(ps_ready, 1)
            for n, m in enumerate((8, 8, 5)):
                for s in range(8 * n, 8 * n + m):
                    c = s * P if s < 16 else PAST + 1 + (s - 16) * P
                    w = P if s < 20 else NCMP
                    ins = turn(bank[0:w, (5, 4, 6)[n], (s - 8 * n) * 64:(s - 8 * n + 1) * 64], ps[:, c:c + w])
                ins.then_inc(tp_done, 1)
            pe.wait_ge(tp_ev, TBP)
            with pe.Fori(0, HPG - 1) as j:
                attend(j, False)
            attend(HPG - 1, True)
            def m3(k, i=None):
                x = ((xh, xl), (vch, vcl), (oth, otl))[0 if k < 4 else k // 2 - 1]
                unit(U_M3 + k, *x, i, 8)

            for k in range(1, 8):
                if k == 2:
                    pe.wait_ge(o64_ready, 1)
                    turn(bank[:, 7, 0:64], o64[:, :]).then_inc(o64_tp, 1)
                    pe.wait_ge(o_lo, 1 + HPG)
                    pe.wait_ge(os_lo, 1)
                if k == 6:
                    pe.wait_ge(os_lo, 1)
                m3(k)
            with pe.Fori(1, 4) as i:
                for k in range(8):
                    m3(k, i)
            for j in range(DC):
                unit(U_M4 + j, mh, ml, ready=ml_done if j == 0 else None)
            ffn(U_F2, 2, DFC)
            def turn_y(t, chunks):
                p = P if t < QT else DB
                for c in chunks:
                    ins = turn(flat(t + 2, D, p)[:, c * P:(c + 1) * P], xg[:, c, t * P:t * P + p])
                return ins

            pe.wait_ge(acc_free, group(U_END - 1))
            for t in range(3):
                if t == 0:
                    pe.wait_ge(xg_ready, DC - 1)
                turn_y(t, range(DC - 1))
            pe.wait_ge(ssq_ready, 4)
            pe.wait_ge(acc_free, group(U_END - 1) + 1)
            pe.matmul(bank[:, 2, QT:QT + 1], ssq[:, 0:P], ones[:, 0:1], start=True, stop=True)
            for t in range(QT + 1):
                p = P if t < QT else DB
                ins = pe.matmul(bank[0:p, 2, t:t + 1], ssq[:, t * P:t * P + p], ones[:, 0:1], start=True, stop=True)
            ins.then_inc(fst_done, 1)
            pe.wait_ge(xg_ready, DC)
            for t in range(QT + 1):
                if t == 3:
                    pe.wait_ge(fms_ready, 1)
                if t >= 4:
                    pe.wait_ge(y_ev, t - 3)
                turn_y(t, (DC - 1,) if t < 3 else range(DC)).then_inc(y_tp, 1)


_KV = (2, KVH, HD)
_OUTS = [('y_prompt', (1, SEQ, D)), ('y_sample', (DB, 1, D)), ('cmp_kv_prompt', (1, 1, SEQ) + _KV), ('sel_kv_prompt', (1, 1, SEQ) + _KV),
         ('win_kv_prompt', (1, 1, SEQ) + _KV), ('conv_prompt', (1, 1, 2, DCV)), ('cmp_kv_sample', (1, DB, 1) + _KV),
         ('sel_kv_sample', (1, DB, 1) + _KV), ('win_kv_sample', (1, DB, SEQ) + _KV), ('conv_sample', (1, DB, 2, DCV))]


def constants():
    f = np.float32
    c = {}
    c["c_ident"] = np.eye(P, dtype=f)
    c["c_sub"] = (np.arange(P) % 8).astype(f)[:, None]
    pos = np.concatenate([np.arange(SEQ), np.full(DB, PAST)]).astype(f)
    freq = np.power(10000.0, -np.arange(HD // 2) * (2.0 / HD)).astype(f)
    ang = (pos[None, :] * freq[:, None]).astype(f)
    cos, sin = np.cos(ang).astype(f), np.sin(ang).astype(f)
    c["c_cs"] = np.stack([np.tile(cos, (4, 1)), np.concatenate([sin, -sin, sin, -sin])], 1)
    q = np.arange(P)
    tri = np.zeros((P, SEQ), f)
    tri[:, SEQ - P:] = np.where(q[None, :] <= q[:, None], 0, NEG)
    c["c_tri"] = tri
    tok = np.arange(QT)[None, :] * P + q[:, None]
    end = np.arange(PCMP) * CH + 2 * CH - 1
    c["c_cmask"] = np.where(end[None, None, :] <= tok[:, :, None], 0, NEG).astype(f)
    c["c_valid"] = (tok >= end[0]).astype(f)
    start = np.arange(NCMP)[:, None] * CH
    jb = np.arange(NSEL)[None, :] * 64
    c["c_mcs"] = ((start < jb + 64) & (start + 2 * CH > jb)).astype(f)
    r = np.arange(64)
    c["c_e16"] = (r[None, :] // HPG == np.arange(16)[:, None]).astype(f)
    c["c_e8"] = (r[None, :] // NH == np.arange(DB)[:, None]).astype(f)
    c["c_dmask"] = (r[:, None] // HPG == np.arange(DB * KVH)[None, :]).astype(f)
    c["c_gmask"] = (r[:, None] // HPG % KVH == np.arange(KVH)[None, :]).astype(f)
    n = np.arange(NSEL)
    c["c_tie"] = np.broadcast_to((n[None, :] < n[:, None]).astype(f), (16, NSEL, NSEL)).copy()
    return c


def kernel(**inputs):
    import numpy as _np
    import concourse.bacc as _bacc
    from concourse import mybir as _mybir
    from concourse.bass_utils import run_bass_kernel_spmd as _run

    nc = _bacc.Bacc("TRN2", target_bir_lowering=False, num_devices=1)
    arrays, aps = {}, {}
    for name, v in list(inputs.items()) + list(constants().items()):
        v = _np.ascontiguousarray(v)
        arrays[name] = v
        aps[name] = nc.dram_tensor(name, v.shape, _mybir.dt.from_np(v.dtype), kind="ExternalInput").ap()
    for name, shape in _OUTS:
        aps[name] = nc.dram_tensor(name, shape, _mybir.dt.float32, kind="ExternalOutput").ap()
    build(nc, aps)
    r = _run(nc, [arrays], core_ids=[0])
    return tuple(r.results[0][name] for name, _ in _OUTS)
```
